# Optimizing a Trainium2 kernel written in Bass

```python
import math
import jax, jax.numpy as jnp
from jax import lax
import numpy as np

D_MODEL = 1024
BATCH = 1
SEQ = 128
DEPTH = 4
DEC_BATCH = 1
DEC_SEQ = 256
PAST_LEN = 128

GRID_W = 64
N_MIXERS = 3
N_A = (DEPTH + 2) // 3
N_B = (DEPTH + 1) // 3
N_C = DEPTH // 3
N_MOD = 9
D_FF = ((8 * D_MODEL // 3 + 127) // 128) * 128
EPS = 1e-6
H_A = D_MODEL // 128
DK_A = 128
DV_A = 128
INNER_A = H_A * DV_A
CONV_K = 5
CHUNK = 64
H_B = D_MODEL // 128
DH_B = 64
Q_BLOCK = 128
ROPE_BASE = 10000.0
POOL_WINDOWS = (2, 4, 8, 16)
POOL_GW = D_MODEL // 4

kernel_name = 'hybrid_diffusion_prefix_trunk_step'

F32 = jnp.float32

def _rms(x, g):
    xf = x.astype(F32)
    y = xf * lax.rsqrt(jnp.mean(xf * xf, axis=-1, keepdims=True) + EPS) * g.astype(F32)
    return y.astype(x.dtype)

def _l2(x):
    xf = x.astype(F32)
    return xf * lax.rsqrt(jnp.sum(xf * xf, axis=-1, keepdims=True) + EPS)

def _modulation(cond, w, b):
    m = jax.nn.silu(cond) @ w + b
    return m.reshape(cond.shape[0], 1, N_MOD, D_MODEL)

def _adanorm(x, g, shift, scale):
    return _rms(x, g) * (1.0 + scale) + shift

def _half_ffn(x, m, j0, g, wg, wu, wd):
    h = _adanorm(x, g, m[:, :, j0], m[:, :, j0 + 1])
    f = (jax.nn.silu(h @ wg) * (h @ wu)) @ wd
    return x + 0.5 * m[:, :, j0 + 2] * f

def _dwconv_centred(x, w):
    k, ch = w.shape
    return lax.conv_general_dilated(x, w[:, None, :].astype(x.dtype), window_strides=(1,),
                                    padding=[(k // 2, k // 2)],
                                    dimension_numbers=('NWC', 'WIO', 'NWC'),
                                    feature_group_count=ch)

def _chunk_gated_delta(q, k, v, g, beta, s0):
    b, l, h, dk = q.shape
    dv = v.shape[-1]
    n = l // CHUNK
    ch = lambda t: t.reshape(b, n, CHUNK, h, t.shape[-1]).transpose(1, 0, 3, 2, 4)
    cg = lambda t: t.reshape(b, n, CHUNK, h).transpose(1, 0, 3, 2)
    q, k, v = ch(q) * (dk ** -0.5), ch(k), ch(v)
    gcum = jnp.cumsum(cg(g), axis=-1)
    beta = cg(beta)
    idx = jnp.arange(CHUNK)
    incl = idx[:, None] >= idx[None, :]
    strict = idx[:, None] > idx[None, :]
    diff = gcum[..., :, None] - gcum[..., None, :]
    decay = jnp.where(incl, jnp.exp(jnp.where(incl, diff, 0.0)), 0.0)
    kb = k * beta[..., None]
    lmat = jnp.where(strict, jnp.einsum('nbhid,nbhjd->nbhij', kb, k) * decay, 0.0)
    amat = lmat + jnp.eye(CHUNK, dtype=F32)
    rhs = jnp.concatenate([v * beta[..., None], kb * jnp.exp(gcum)[..., None]], axis=-1)
    sol = lax.linalg.triangular_solve(amat, rhs, left_side=True, lower=True, unit_diagonal=True)
    u, w = sol[..., :dv], sol[..., dv:]
    attn = jnp.einsum('nbhid,nbhjd->nbhij', q, k) * decay
    qg = q * jnp.exp(gcum)[..., None]
    kd = k * jnp.exp(gcum[..., -1:] - gcum)[..., None]
    glast = jnp.exp(gcum[..., -1])

    def step(s, xs):
        u_i, w_i, attn_i, qg_i, kd_i, gl_i = xs
        v_new = u_i - jnp.einsum('bhcd,bhde->bhce', w_i, s)
        o = jnp.einsum('bhcd,bhde->bhce', qg_i, s) + jnp.einsum('bhij,bhje->bhie', attn_i, v_new)
        s = s * gl_i[..., None, None] + jnp.einsum('bhcd,bhce->bhde', kd_i, v_new)
        return s, o

    s_fin, o = lax.scan(step, s0, (u, w, attn, qg, kd, glast))
    o = o.transpose(1, 0, 3, 2, 4).reshape(b, l, h, dv)
    return o, s_fin

def _gated_deltanet(h, w_in, conv_w, a_log, dt_bias, norm_g, w_out, s0_f, s0_b):
    b, l, _ = h.shape
    proj = h @ w_in
    qkv = jax.nn.silu(_dwconv_centred(proj[..., :3 * INNER_A], conv_w))
    z = proj[..., 3 * INNER_A:4 * INNER_A].reshape(b, l, H_A, DV_A)
    ab = proj[..., 4 * INNER_A:].astype(F32).reshape(b, l, 2, 2, H_A)
    q = _l2(qkv[..., :INNER_A].reshape(b, l, H_A, DK_A))
    k = _l2(qkv[..., INNER_A:2 * INNER_A].reshape(b, l, H_A, DK_A))
    v = qkv[..., 2 * INNER_A:].astype(F32).reshape(b, l, H_A, DV_A)
    g = -jnp.exp(a_log.astype(F32)) * jax.nn.softplus(ab[:, :, :, 0] + dt_bias.astype(F32))
    beta = jax.nn.sigmoid(ab[:, :, :, 1])
    o_f, s_f = _chunk_gated_delta(q, k, v, g[:, :, 0], beta[:, :, 0], s0_f.astype(F32))
    rev = lambda t: jnp.flip(t, axis=1)
    o_b, s_b = _chunk_gated_delta(rev(q), rev(k), rev(v), rev(g[:, :, 1]), rev(beta[:, :, 1]),
                                  s0_b.astype(F32))
    o = o_f + rev(o_b)
    o = _rms(o, norm_g) * jax.nn.silu(z.astype(F32))
    y = o.reshape(b, l, INNER_A).astype(h.dtype) @ w_out
    return y, s_f, s_b

def _rope_1d(x, pos):
    nf = x.shape[-1] // 2
    inv = ROPE_BASE ** (-jnp.arange(nf, dtype=F32) / nf)
    ang = pos.astype(F32)[:, None] * inv
    cos = jnp.cos(ang)[None, :, None, None, :]
    sin = jnp.sin(ang)[None, :, None, None, :]
    xf = x.astype(F32)
    x1, x2 = xf[..., :nf], xf[..., nf:]
    return jnp.concatenate([x1 * cos - x2 * sin, x2 * cos + x1 * sin], axis=-1).astype(x.dtype)

def _axial_rope(x, row, col):
    half = x.shape[-1] // 2
    return jnp.concatenate([_rope_1d(x[..., :half], row), _rope_1d(x[..., half:], col)], axis=-1)

def _diff_qkv(h, w_qkv):
    b, l, _ = h.shape
    qkv = (h @ w_qkv).reshape(b, l, 3, H_B, 2, DH_B)
    return qkv[:, :, 0], qkv[:, :, 1], qkv[:, :, 2].reshape(b, l, H_B, 2 * DH_B)

def _diff_lambda(lam_p, lam_init):
    lp = lam_p.astype(F32)
    return jnp.exp(jnp.sum(lp[0] * lp[1])) - jnp.exp(jnp.sum(lp[2] * lp[3])) + lam_init

def _diff_attend(q, k, v, lam, lam_init, norm_g, w_out):
    b, lq = q.shape[:2]
    nb = lq // Q_BLOCK
    qb = jnp.moveaxis(q.reshape(b, nb, Q_BLOCK, H_B, 2, DH_B), 1, 0)
    scale = DH_B ** -0.5

    def blk(qi):
        s = jnp.einsum('bqhcd,bkhcd->bhcqk', qi, k).astype(F32) * scale
        p = jax.nn.softmax(s, axis=-1)
        a = (p[:, :, 0] - lam * p[:, :, 1]).astype(v.dtype)
        return jnp.einsum('bhqk,bkhe->bqhe', a, v)

    o = lax.map(blk, qb)
    o = jnp.moveaxis(o, 0, 1).reshape(b, lq, H_B, 2 * DH_B)
    o = _rms(o, norm_g) * (1.0 - lam_init)
    return o.reshape(b, lq, H_B * 2 * DH_B) @ w_out

def _pool_mixer(h, w_pool, scale):
    b, l, d = h.shape
    hf = h.astype(F32)
    cs = jnp.concatenate([jnp.zeros((b, 1, d), F32), jnp.cumsum(hf, axis=1)], axis=1)
    t = jnp.arange(l)
    parts = []
    for gi, win in enumerate(POOL_WINDOWS):
        sl = slice(gi * POOL_GW, (gi + 1) * POOL_GW)
        lo = jnp.clip(t - win // 2, 0, l)
        hi = jnp.clip(t + win // 2, 0, l)
        cnt = (hi - lo).astype(F32)[None, :, None]
        csg = cs[:, :, sl]
        parts.append((csg[:, hi] - csg[:, lo]) / cnt - hf[:, :, sl])
    dlt = jnp.stack(parts, axis=2)
    y = jnp.einsum('blgc,gce->blge', dlt, w_pool.astype(F32)).reshape(b, l, d) * scale.astype(F32)
    return y.astype(h.dtype)

def setup_inputs(seed: int = 0) -> dict:
    key = jax.random.key(seed)
    ks = iter(jax.random.split(key, 40))
    D = D_MODEL

    def nrm(shape, s=1.0):
        return jax.random.normal(next(ks), shape, F32) * s

    inp = {}
    inp['x_prompt'] = nrm((BATCH, SEQ, D))
    inp['x_sample'] = nrm((DEC_BATCH, DEC_SEQ, D))
    inp['state_a'] = nrm((DEC_BATCH, N_A, 2, H_A, DK_A, DV_A), 0.1)
    inp['cache_k'] = nrm((DEC_BATCH, N_B, PAST_LEN, H_B, 2 * DH_B))
    inp['cache_v'] = nrm((DEC_BATCH, N_B, PAST_LEN, H_B, 2 * DH_B))
    inp['c'] = nrm((DEC_BATCH, D))
    inp['c_ctx'] = nrm((D,))
    inp['w_mod'] = nrm((DEPTH, D, N_MOD * D), 0.5 * D ** -0.5)
    inp['b_mod'] = nrm((DEPTH, N_MOD * D), 0.01)
    inp['norm_g'] = 1.0 + nrm((DEPTH, 3, D), 0.02)
    inp['ffn_wg'] = nrm((DEPTH, 2, D, D_FF), D ** -0.5)
    inp['ffn_wu'] = nrm((DEPTH, 2, D, D_FF), D ** -0.5)
    inp['ffn_wd'] = nrm((DEPTH, 2, D_FF, D), D_FF ** -0.5)
    inp['a_w_in'] = nrm((N_A, D, 4 * INNER_A + 4 * H_A), D ** -0.5)
    inp['a_conv'] = nrm((N_A, CONV_K, 3 * INNER_A), CONV_K ** -0.5)
    a_val = jax.random.uniform(next(ks), (N_A, 2, H_A), F32, minval=1.0, maxval=16.0)
    inp['a_A_log'] = jnp.log(a_val)
    dt = jnp.exp(jax.random.uniform(next(ks), (N_A, 2, H_A), F32,
                                    minval=math.log(1e-3), maxval=math.log(1e-1)))
    inp['a_dt_bias'] = dt + jnp.log(-jnp.expm1(-dt))
    inp['a_norm_g'] = 1.0 + nrm((N_A, DV_A), 0.02)
    inp['a_w_out'] = nrm((N_A, INNER_A, D), INNER_A ** -0.5)
    inp['b_w_qkv'] = nrm((N_B, D, 3 * H_B * 2 * DH_B), D ** -0.5)
    inp['b_lam'] = nrm((N_B, 4, DH_B), 0.1)
    inp['b_norm_g'] = 1.0 + nrm((N_B, 2 * DH_B), 0.02)
    inp['b_w_out'] = nrm((N_B, H_B * 2 * DH_B, D), (H_B * 2 * DH_B) ** -0.5)
    inp['c_w_pool'] = nrm((N_C, 4, POOL_GW, POOL_GW), POOL_GW ** -0.5)
    inp['c_scale'] = 1.0 + nrm((N_C, D), 0.02)
    inp['final_g'] = 1.0 + nrm((D,), 0.02)
    return inp

def reference(x_prompt, x_sample, state_a, cache_k, cache_v, c, c_ctx, w_mod, b_mod, norm_g,
              ffn_wg, ffn_wu, ffn_wd, a_w_in, a_conv, a_A_log, a_dt_bias, a_norm_g, a_w_out,
              b_w_qkv, b_lam, b_norm_g, b_w_out, c_w_pool, c_scale, final_g):
    bp, lp, _ = x_prompt.shape
    bs, ls, _ = x_sample.shape
    rows = ls // GRID_W
    row_pos = jnp.repeat(jnp.arange(rows), GRID_W)
    col_pos = jnp.tile(jnp.arange(GRID_W), rows)
    xp, xs = x_prompt, x_sample
    new_sa, new_k, new_v = [], [], []
    for i in range(DEPTH):
        kind, slot = i % N_MIXERS, i // N_MIXERS
        mp = _modulation(c_ctx[None, :], w_mod[i], b_mod[i])
        ms = _modulation(c, w_mod[i], b_mod[i])
        xp = _half_ffn(xp, mp, 0, norm_g[i, 0], ffn_wg[i, 0], ffn_wu[i, 0], ffn_wd[i, 0])
        xs = _half_ffn(xs, ms, 0, norm_g[i, 0], ffn_wg[i, 0], ffn_wu[i, 0], ffn_wd[i, 0])
        hp = _adanorm(xp, norm_g[i, 1], mp[:, :, 3], mp[:, :, 4])
        hs = _adanorm(xs, norm_g[i, 1], ms[:, :, 3], ms[:, :, 4])
        if kind == 0:
            wa = (a_w_in[slot], a_conv[slot], a_A_log[slot], a_dt_bias[slot], a_norm_g[slot], a_w_out[slot])
            z0 = jnp.zeros((bp, H_A, DK_A, DV_A), F32)
            yp, s_f, s_b = _gated_deltanet(hp, *wa, z0, z0)
            ys, _, _ = _gated_deltanet(hs, *wa, state_a[:, slot, 0], state_a[:, slot, 1])
            new_sa.append(jnp.stack([s_f, s_b], axis=1))
        elif kind == 1:
            lam_init = 0.8 - 0.6 * math.exp(-0.3 * i)
            lam = _diff_lambda(b_lam[slot], lam_init)
            qp, kp, vp = _diff_qkv(hp, b_w_qkv[slot])
            yp = _diff_attend(qp, kp, vp, lam, lam_init, b_norm_g[slot], b_w_out[slot])
            qs, ks_, vs = _diff_qkv(hs, b_w_qkv[slot])
            qs = _axial_rope(qs, row_pos, col_pos)
            ks_ = _axial_rope(ks_, row_pos, col_pos)
            ck = cache_k[:, slot].reshape(bs, cache_k.shape[2], H_B, 2, DH_B).astype(ks_.dtype)
            k_all = jnp.concatenate([ks_, ck], axis=1)
            v_all = jnp.concatenate([vs, cache_v[:, slot].astype(vs.dtype)], axis=1)
            ys = _diff_attend(qs, k_all, v_all, lam, lam_init, b_norm_g[slot], b_w_out[slot])
            new_k.append(kp.reshape(bp, lp, H_B, 2 * DH_B))
            new_v.append(vp)
        else:
            yp = _pool_mixer(hp, c_w_pool[slot], c_scale[slot])
            ys = _pool_mixer(hs, c_w_pool[slot], c_scale[slot])
        xp = xp + mp[:, :, 5] * yp
        xs = xs + ms[:, :, 5] * ys
        xp = _half_ffn(xp, mp, 6, norm_g[i, 2], ffn_wg[i, 1], ffn_wu[i, 1], ffn_wd[i, 1])
        xs = _half_ffn(xs, ms, 6, norm_g[i, 2], ffn_wg[i, 1], ffn_wu[i, 1], ffn_wd[i, 1])
    y_prompt = _rms(xp, final_g)
    y_sample = _rms(xs, final_g)
    state_a_new = jnp.stack(new_sa, axis=1)
    cache_k_new = jnp.stack(new_k, axis=1)
    cache_v_new = jnp.stack(new_v, axis=1)
    return (y_prompt, y_sample, state_a_new, cache_k_new, cache_v_new)


_drawn_inputs = setup_inputs


def setup_inputs(seed=0):
    import zlib

    import numpy as np

    out = dict(_drawn_inputs(seed))
    spreads = {}
    factors = {'a_norm_g': 8.0, 'b_norm_g': 92.78, 'c_scale': 138.377, 'final_g': 21.105}
    for name, (base, spread) in spreads.items():
        noise = np.random.default_rng([zlib.crc32(name.encode()), seed]).standard_normal(out[name].shape)
        drawn = base * np.exp(spread * noise) if base else spread * noise
        out[name] = __import__('jax').numpy.asarray(drawn.astype(out[name].dtype))
    for name, factor in factors.items():
        out[name] = (out[name] * factor).astype(out[name].dtype)
    return out
```

```python
import math

import numpy as np
import concourse.bass as bass
from concourse import mybir
from concourse.alu_op_type import AluOpType as ALU

F32 = mybir.dt.float32
F32R = mybir.dt.float32r
ACT = mybir.ActivationFunctionType
AX = mybir.AxisListType

P = 128
D = 1024
KT = D // P
DEPTH = 4
TP, TS = 128, 256
T = TP + TS
NT = T // P
D_FF = 2816
FT = D_FF // P
N_MOD = 9
EPS = 1e-6
HEADS = D // P
CONV = 5
PAST = 128
DH = 64
CHANNEL_SPANS = ((0, TP), (TP, T))
PART = KT * P
POOL_WINDOWS = (2, 4, 8, 16)
GROUP = 4
LEVELS = 7
AB = 4 * HEADS

MOD_TILES = 2
MOD_UNITS = N_MOD * KT // MOD_TILES
MOD_PROLOGUE = 3 * KT // MOD_TILES
MOD_PER_FFN = 18
MOD_EXTRA = (MOD_UNITS - MOD_PROLOGUE - MOD_PER_FFN) // 2

COL_NORM_G = 0
COL_MOD_B = COL_NORM_G + DEPTH * 3 * KT
COL_CONV = COL_MOD_B + DEPTH * N_MOD * KT
COL_A_NORM = COL_CONV + 2 * 24 * CONV
COL_B_NORM = COL_A_NORM + 2
COL_C_SCALE = COL_B_NORM + 1
COLS = COL_C_SCALE + KT
ROW_A_LOG, ROW_DT, ROW_LAM, ROWS = 0, 32, 64, 64 + 4 * DH

CONV_PAD = CONV // 2
CONV_W = CONV_PAD + TP + CONV_PAD + TS + CONV_PAD
CONV_OUT = CONV_W - 2 * CONV_PAD
POOL_PAD = max(POOL_WINDOWS) // 2
POOL_W = POOL_PAD + TP + POOL_PAD + TS + POOL_PAD
POOL_OUT = POOL_W - 2 * POOL_PAD
SCRATCH_W = 392
LAM_INIT = 0.8 - 0.6 * math.exp(-0.3)
AT_NEG_MAX, AT_SUM, AT_RECIP, AT_SCALED, AT_LAM, AT_NEG_LAM, AT_NORM = 16, 20, 24, 28, 30, 32, 33


def weight_phases():
    mixers = (("a_in", 11, 3), ("a_out", 3, 2)), (("b_in", 8, 3), ("b_out", 3, 2)), (("c_in", 1, 2),)
    out = []
    for layer in range(DEPTH):
        out.append(("ffn", FT, 3, 2 * layer))
        out += [(name, units, last, layer) for name, units, last in mixers[layer % 3]]
        out.append(("ffn", FT, 3, 2 * layer + 1))
    return out


class Phase:

    def __init__(self, name, units, last_parts, index, before):
        self.name, self.units, self.last_parts, self.index = name, units, last_parts, index
        self.n0 = before.n0 + before.units if before else 0
        self.parts0 = before.parts0 + 3 * before.units - (3 - before.last_parts) if before else 0
        self.missing0 = 3 * self.n0 - self.parts0


class Unit:

    def __init__(self, phase, k, body=0):
        n = phase.n0 + k
        self.phase, self.k = phase, k
        self.n = n + 2 * body
        self.slot = n % 2
        self.landed = 16 * (n // 2 + body + 1)
        self.local = k + 2 * body
        self.parts_before = phase.parts0 + 3 * (k + 2 * body)
        last = k == phase.units - 1
        self.parts = phase.last_parts if last else 3
        self.first_two = isinstance(self.n, int) and self.n < 2

    def split_count(self, q):
        return self.parts_before + q + 1

    def width(self, q):
        return KT * AB if self.phase.name == "a_in" and self.k == self.phase.units - 1 and q == 2 else PART


def build(nc, inp, out, stages=3 * DEPTH):
    phases = []
    for name, units, last, index in weight_phases():
        phases.append(Phase(name, units, last, index, phases[-1] if phases else None))
    if stages < 3 * DEPTH:
        keep = []
        for ph in phases:
            stage = {"f": 3 * (ph.index // 2) + 2 * (ph.index % 2)}.get(ph.name[0], 3 * ph.index + 1)
            if stage < stages:
                keep.append(ph)
        phases = keep
    by_stage = {}
    for ph in phases:
        stage = 3 * (ph.index // 2) + 2 * (ph.index % 2) if ph.name == "ffn" else 3 * ph.index + 1
        by_stage.setdefault(stage, []).append(ph)

    def phase_of(n):
        return next(ph for ph in phases if ph.n0 <= n < ph.n0 + ph.units)

    def following(unit):
        ph = unit.phase
        if isinstance(unit.n, int):
            n = unit.n + 1
            if n >= phases[-1].n0 + phases[-1].units:
                return None
            nxt = phase_of(n)
            return Unit(nxt, n - nxt.n0)
        return None

    def release(unit, q):
        if isinstance(unit.n, int):
            ph = phase_of(unit.n - 2)
        else:
            ph = unit.phase
        which = 2 if ph.name == "b_in" else q
        n = unit.n - 2
        if isinstance(unit.n, int):
            old = Unit(ph, n - ph.n0)
            if q >= old.parts:
                which = 1
        return which, n + 1 - (ph.missing0 if which == 2 else 0)

    def done(unit, q):
        return unit.n + 1 - (unit.phase.missing0 if q == 2 else 0)

    def mod_steps(f, b, first, last):
        if f >= 7:
            return []
        layer = (f + 1) // 2
        if f:
            m0 = MOD_UNITS + MOD_PER_FFN * (f - 1)
        else:
            m0 = MOD_PROLOGUE + MOD_EXTRA
        if not first and not last:
            return [(u, m0 + u + 2 * (b - 1), (m0 + u) % 2, 16 * ((m0 + u - MOD_PROLOGUE) // 2 + 1 + b), layer) for u in range(2)]
        if f:
            return []
        start = MOD_PROLOGUE if first else MOD_UNITS - MOD_EXTRA
        return [(min(i, 1), start + i, (start + i) % 2, 16 * ((start + i - MOD_PROLOGUE) // 2 + 2), layer) for i in range(MOD_EXTRA)]

    NORMS = stages

    def oT_base(layer):
        return KT * layer

    def xT_base(r):
        return KT * (r - (r > 7))

    base = nc.sbuf_base + (-nc.sbuf_base) % 64
    top = [base]

    def place(name, shape, dtype=F32, at=None):
        size = int(np.prod(shape[1:])) * 4
        if at is None:
            at = top[0]
            top[0] += size + (-size) % 32
        assert at + size <= nc.sbuf_usable_end, (name, at + size, nc.sbuf_usable_end)
        return nc.alloc_sbuf_tensor_at(name, shape, dtype, offset=at)

    raw = place("raw", [P, 2, 3, PART])
    region_m = top[0]
    mod_raw = place("mod_raw", [P, 2, MOD_TILES, D])
    x = place("x", [P, NT, D])
    region_a = top[0]
    xT_hi = place("xT_hi", [P, KT, T], F32R)
    xT_lo = place("xT_lo", [P, KT, T], F32R)
    gate_bc = place("gate_bc", [P, 2, D])
    ident = place("ident", [P, P])
    ones = place("ones", [P, P])
    tri = place("tri", [P, 2, P])
    cond = place("cond", [P, 2, D])
    rope_tab = place("rope_tab", [P, 2, 2, DH])
    cols = place("cols", [P, COLS])
    rows = place("rows", [P, ROWS])
    modv = place("modv", [P, 2, N_MOD * KT, 2])
    scale_col = place("scale_col", [P, KT, 2])
    gate_col = place("gate_col", [P, KT, 2])
    sumsq = place("sumsq", [P, 24])
    rstd = place("rstd", [P, 24])
    neg_half = place("neg_half", [P, 24])
    bias_eps = place("bias_eps", [P, 1])
    dn_small = place("dn_small", [P, 12, NT, 2, HEADS])
    at_small = place("at_small", [P, 64])
    lam_prod = place("lam_prod", [P, 2, DH])
    region_w = top[0]
    split_hi = place("split_hi", [P, 2, 3, PART], F32R)
    split_lo = place("split_lo", [P, 2, 3, PART], F32R)
    region_r = top[0]
    KB = 1024
    scratch = place("scratch", [P, 4, SCRATCH_W], at=region_r + 48 * KB)
    diag = place("diag", [P, 2, KT, P], at=region_r)
    res_tmp = place("res_tmp", [P, 3, 512], at=region_r + 12 * KB)
    xhat = place("xhat", [P, NT, D], at=region_r + 24 * KB)
    silu_g = place("silu_g", [P, 2, T], at=region_r + 36 * KB)
    hidden = place("hidden", [P, 2, T], at=region_r + 39 * KB)
    hid_hi = place("hid_hi", [P, 2, T], F32R, at=region_r + 42 * KB)
    hid_lo = place("hid_lo", [P, 2, T], F32R, at=region_r + 45 * KB)
    final_row = place("final_row", [P, D], at=region_r)
    mod_junk = place("mod_junk", [P, D], at=region_r + 8 * KB)
    mod_prod = place("mod_prod", [P, 2, D], at=region_r + 24 * KB)
    mod_at = [region_w + 8 * KB * i for i in range(6)] + [region_a + 8 * KB * i for i in range(4)]
    mod_first = [place(f"mod_first{i}", [P, MOD_TILES, D], at=at) for i, at in enumerate(mod_at)]
    level_mask = place("level_mask", [P, 2, LEVELS, P], at=region_m + 8 * KB)
    qkvz = place("qkvz", [P, 4 * HEADS, T], at=region_r)
    dn_o = place("dn_o", [P, NT, HEADS, P], at=region_r + 24 * KB)
    dn_k = place("dn_k", [P, NT, HEADS, P], at=region_a)
    dn_v = place("dn_v", [P, NT, HEADS, P], at=region_a + 12 * KB)
    state = place("state", [P, 2, HEADS, P], at=region_w)
    work = [[place(f"work_{d}_{i}", [P, GROUP, P], at=region_w + (8 + 20 * d + 2 * i) * KB) for i in range(10)]
            for d in range(2)]
    sq_tmp = place("sq_tmp", [P, NT, HEADS, P], at=region_r + 12 * KB)
    at_q = place("at_q", [P, NT, D], at=region_r)
    at_k = place("at_k", [P, NT, D], at=region_r + 12 * KB)
    at_v = place("at_v", [P, NT, D], at=region_r + 24 * KB)
    past_k = place("past_k", [P, D], at=region_r + 36 * KB)
    past_v = place("past_v", [P, D], at=region_r + 40 * KB)
    at_o = place("at_o", [P, NT, HEADS, P], at=region_r)
    rope_a = place("rope_a", [P, D], at=region_r + 44 * KB)
    rope_b = place("rope_b", [P, D], at=region_r + 48 * KB)
    qT = place("qT", [P, HEADS, T], at=region_w)
    kT = place("kT", [P, HEADS, T + PAST], at=region_w + 12 * KB)
    prob = place("prob", [P, 2, 2, T], at=region_w + 28 * KB)
    probT = place("probT", [P, 2, T], at=region_w + 34 * KB)
    hpad = place("hpad", [P, KT, POOL_W], at=region_r)
    pool_tmp = place("pool_tmp", [P, 3, POOL_W], at=region_r + 14 * KB)
    inv_count = place("inv_count", [P, 4, POOL_OUT], at=region_r + 36 * KB)

    ps = [nc.alloc_psum_tensor(f"bank{i}", [P, 512], F32) for i in range(8)]
    BANK_GATE, BANK_UP = 6, 7
    NORM_BANK = (6, 7, 4, 5, 0, 1, 2, 3)
    PROJ_BANK = (6, 7, 5)

    sem = nc.alloc_semaphore
    consts_in = sem("consts_in")
    x_in = sem("x_in")
    cond_in, cond_ready = sem("cond_in"), sem("cond_ready")
    pool_init = sem("pool_init")
    raw_landed = [sem(f"raw_landed{i}") for i in range(2)]
    hi_ready, lo_ready = sem("hi_ready"), sem("lo_ready")
    part_done = [sem(f"part_done{q}") for q in range(3)]
    mod_landed = [sem(f"mod_landed{i}") for i in range(2)]
    mod_first_landed = [sem(f"mod_first_landed{i}") for i in range(len(mod_first))]
    mod_first_sum = {e: sem(f"mod_first_{e}") for e in ("dve", "mult", "act")}
    mod_sum = {e: sem(f"mod_{e}") for e in ("dve", "mult", "act")}
    mask_in = sem("mask_in")
    scale_ready, diag_ready = sem("scale_ready"), sem("diag_ready")
    gate_mm, gate_ready = sem("gate_mm"), sem("gate_ready")
    res_prod, res_pool, res_dve = sem("res_prod"), sem("res_pool"), sem("res_dve")
    sumsq_ready, rstd_ready, xhat_ready = sem("sumsq_ready"), sem("rstd_ready"), sem("xhat_ready")
    tr_ready, xn_ready, xT_ready = sem("tr_ready"), sem("xn_ready"), sem("xT_ready")
    silu_done, prod_done, hid_hi_done, hid_done = (sem(s) for s in ("silu_done", "prod_done", "hid_hi_done", "hid_done"))
    dve_seq, act_seq, pool_seq = sem("dve_seq"), sem("act_seq"), sem("pool_seq")
    y_ready, stored = sem("y_ready"), sem("stored")
    oss_ready, orstd_ready, ohat_ready = sem("oss_ready"), sem("orstd_ready"), sem("ohat_ready")
    otr_ready, on_ready, ohi_ready, oT_ready = sem("otr_ready"), sem("on_ready"), sem("ohi_ready"), sem("oT_ready")
    osq_ready = sem("osq_ready")
    pad_zero, tile_used, conv_step, conv_silu = (sem(n) for n in ("pad_zero", "tile_used", "conv_step", "conv_silu"))
    sq_ready, ss_done, r_ready, unit_ready, z_ready = (sem(n) for n in ("sq_ready", "ss_done", "r_ready", "unit_ready", "z_ready"))
    tokT_done, tok_v, tok_k = sem("tokT_done"), sem("tok_v"), sem("tok_k")
    ab_in, ab_exp, g_ready, gc_done = sem("ab_in"), sem("ab_exp"), sem("g_ready"), sem("gc_done")
    decay_in, decay_out, small_ready = sem("decay_in"), sem("decay_out"), sem("small_ready")
    state_in, state_set, state_stored = sem("state_in"), sem("state_set"), sem("state_stored")
    dn_mm, dn_dve, dn_act, dn_pool, dn_sum = ([sem(f"dn_{e}{d}") for d in range(2)] for e in ("mm", "dve", "act", "pool", "sum"))
    qkv_copied, past_in, roped, lam_ready, lam_exp = (sem(s) for s in ("qkv_copied", "past_in", "roped", "lam_ready", "lam_exp"))
    cache_out = sem("cache_out")
    head_tr, q_head, k_head = sem("head_tr"), sem("q_head"), sem("k_head")
    score_done, max_done, exp_done, prob_done = (sem(s) for s in ("score_done", "max_done", "exp_done", "prob_done"))
    pT_done, pT_copied, ao_done, ao_copied = (sem(s) for s in ("pT_done", "pT_copied", "ao_done", "ao_copied"))
    hpad_zero, hpad_ready, count_in = sem("hpad_zero"), sem("hpad_ready"), sem("count_in")

    CONSTS = 5

    def f32(ap):
        return ap.bitcast(F32)

    def vec_of(r):
        return r // 3 % 2, 3 * KT * (r % 3)

    def mod_needed(r):
        layer, which = divmod(r, 3)
        return MOD_UNITS * layer + (which + 1) * 3 * KT // MOD_TILES

    def mod_operand(m):
        if m < len(mod_first):
            return mod_first[m][:], mod_first_landed[m], 16
        return mod_raw[:, m % 2], mod_landed[m % 2], 16 * ((m - len(mod_first)) // 2 + 1)

    def in_prologue(m):
        return isinstance(m, int) and m < MOD_PROLOGUE

    def mod_count(which, m, i=0):
        if isinstance(m, int) and m <= MOD_PROLOGUE and not (m == MOD_PROLOGUE and i):
            return mod_first_sum[which], (3 if which == "dve" else 1) * m + i
        return mod_sum[which], 2 * (m - MOD_PROLOGUE) + i

    def mod_column(layer, unit, t, c):
        return modv[:, layer % 2, bass.ds(MOD_TILES * unit + t, 1), c:c + 1].rearrange("p t c -> p (t c)")

    def mod_dve(eng, weights, landed, count, m, layer, unit):
        eng.wait_ge(landed, count)
        for i, (t, c) in enumerate(((0, 0), (1, 0), (0, 1)) if in_prologue(m) else ((0, 0), (1, 0))):
            if not (isinstance(m, int) and m == 0 and i == 0):
                eng.wait_ge(*mod_count("dve", m, i))
            eng.scalar_tensor_tensor(mod_junk[:], weights[:, t], 1.0, cond[:, c], ALU.mult, ALU.mult,
                                     accum_out=mod_column(layer, unit, t, c)).then_inc(mod_count("dve", m, 1)[0], 1)

    def mod_pool(eng, weights, landed, count, m):
        eng.wait_ge(landed, count)
        for i, t in enumerate((1,) if in_prologue(m) else (0, 1)):
            if not in_prologue(m):
                if isinstance(m, int) and m == MOD_PROLOGUE:
                    eng.wait_ge(*mod_count("act", m))
                else:
                    eng.wait_ge(*mod_count("act", m - 1, i + 1))
            elif m >= 2:
                eng.wait_ge(*mod_count("act", m - 1))
            buf = mod_prod[:, m % 2 if in_prologue(m) else i]
            eng.tensor_tensor(buf, weights[:, t], cond[:, 1], ALU.mult).then_inc(mod_count("mult", m, 1)[0], 1)

    def mod_act(eng, m, layer, unit):
        for i, t in enumerate((1,) if in_prologue(m) else (0, 1)):
            eng.wait_ge(*mod_count("mult", m, i + 1))
            buf = mod_prod[:, m % 2 if in_prologue(m) else i]
            eng.activation(buf, buf, ACT.Copy, accum_out=mod_column(layer, unit, t, 1)).then_inc(mod_count("act", m, 1)[0], 1)

    def mod_before(r):
        ffns = 2 * (r // 3) + (r % 3 + 1) // 2
        return MOD_UNITS + MOD_PER_FFN * (min(ffns, 7) - 1) if ffns else MOD_PROLOGUE

    def bodies(eng, count, body):
        body(0, True, False)
        with eng.Fori(1, count - 1) as b:
            body(b, False, False)
        body(count - 1, False, True)

    class Steps:

        def __init__(self, eng, s):
            self.eng, self.s, self.n = eng, s, 0

        def settle(self, ins):
            self.n += 1
            ins.then_inc(self.s, 1)
            self.eng.wait_ge(self.s, self.n)

    PAIRS = [((0, 0), 0), ((0, 0), 1), ((1, 2), 0), ((1, 2), 1), ((2, 1), 0), ((2, 1), 1)]
    (W_Y, W_E, W_A, W_ATT, W_T, W_U, W_VB, W_VN, W_MASK) = range(9)
    MM_D, MM_KQ, MM_Y0, MM_U6, MM_KS, MM_QS, MM_VN, MM_OI, MM_DS = 1, 2, 3, 22, 23, 24, 25, 26, 27
    mm_y = lambda lev: 3 * lev + 1 if lev else MM_Y0
    mm_z = lambda lev: 3 * lev + 3
    mm_u = lambda lev: 3 * lev + 5 if lev < LEVELS - 1 else MM_U6
    DV_G4, DV_ARG, DV_MIN, DV_A, DV_ATT, DV_KS, DV_R, DV_QS, DV_VS, DV_O, DV_STATE = 1, 2, 3, 4, 5, 20, 21, 22, 23, 24, 25
    dv_y = lambda lev: 2 * lev + 6
    dv_t = lambda lev: 2 * lev + 7
    AC_EXP, AC_VN = 1, 9
    ac_u = lambda lev: lev + 2
    PO_E, PO_VB, PO_STATE = 1, 4, 10
    po_m = lambda lev: lev + 2 if lev < 2 else lev + 3
    N_MM, N_DV, N_AC, N_PO = 27, 25, 9, 10
    SM_X, SM_G, SM_GC, SM_TOTAL, SM_EG, SM_GLAST, SM_EKD, SM_BEG, SM_BETA, SM_B, SM_ABS = range(11)

    def small(which, c, d, quad):
        v = dn_small[:, which, c, d, GROUP * quad:GROUP * quad + GROUP]
        return v.rearrange("p (h o) -> p h o", o=1).to_broadcast([P, GROUP, P])

    def per_head(ap):
        return ap.rearrange("p (o c) -> p o c", o=1).to_broadcast([P, GROUP, P])

    def writes_first(pair, d):
        return d == 0 if pair < 2 else pair < 4

    def heads_of(quad):
        return slice(GROUP * quad, GROUP * quad + GROUP)

    def tail_index(layer):
        return layer - (layer > 2)

    block = nc.Block()
    block.__enter__()

    @block.sync
    def _(sp):
        def load_unit(unit):
            if not unit.first_two:
                if isinstance(unit.n, int):
                    ph = phase_of(unit.n - 2)
                    old = Unit(ph, unit.n - 2 - ph.n0)
                    sp.wait_ge(lo_ready, old.split_count(old.parts - 1))
                else:
                    sp.wait_ge(lo_ready, unit.parts_before - 3)
            ph = unit.phase
            width = sum(unit.width(q) for q in range(unit.parts))
            dst = raw[:, unit.slot].rearrange("p q c -> p (q c)")[:, 0:width]
            if ph.name == "ffn":
                src = inp["ffn_w"][ph.index, bass.ds(unit.local, 1)].rearrange("u p c -> (u p) c")
            elif ph.name == "a_in":
                src = inp["a_in_w"][ph.index // 3, bass.ds(unit.local, 1)].rearrange("u p c -> (u p) c")[:, 0:width]
            elif ph.name == "b_in":
                src = inp["b_in_w"][bass.ds(unit.local, 1)].rearrange("u p c -> (u p) c")
            elif ph.name == "a_out":
                src = inp["a_out_w"][ph.index // 3, :, unit.k * 3 * PART:unit.k * 3 * PART + width]
            elif ph.name == "b_out":
                src = inp["b_out_w"][:, unit.k * 3 * PART:unit.k * 3 * PART + width]
            else:
                src = inp["c_w"]
            sp.dma_start(dst, src).then_inc(raw_landed[unit.slot], 16)

        def load_mod(m, slot, layer, unit):
            sp.wait_ge(*mod_count("dve", m - 1))
            sp.wait_ge(*mod_count("mult", m - 1))
            src = inp["mod_w"][layer, bass.ds(unit, 1)].rearrange("u p c -> (u p) c")
            sp.dma_start(mod_raw[:, slot].rearrange("p t c -> p (t c)"), src).then_inc(mod_landed[slot], 16)

        sp.dma_start(cond[:].rearrange("p c k -> p (c k)"), inp["cond"].to_broadcast([P, 2 * D])).then_inc(cond_in, 16)
        for m in range(MOD_PROLOGUE):
            dst, landed, _ = mod_operand(m)
            sp.dma_start(dst.rearrange("p t c -> p (t c)"), inp["mod_w"][0, m]).then_inc(landed, 16)
            if m >= MOD_PROLOGUE - 2:
                load_unit(Unit(phases[0], m - MOD_PROLOGUE + 2))
        for stage in range(NORMS):
            for ph in by_stage[stage]:
                if ph.name == "ffn":
                    f = ph.index

                    def load_body(b, first, last):
                        if f == 1 and first:
                            for d in range(2):
                                sp.wait_ge(dn_pool[d], 6 * N_PO)
                        for u in range(2):
                            if not (ph.n0 == 0 and first):
                                load_unit(Unit(ph, u if first else ph.units - 2 + u if last else u, b if not (first or last) else 0))
                            for step, m, slot, _, layer in mod_steps(f, b, first, last):
                                if step == u:
                                    load_mod(m, slot, layer, m - MOD_UNITS * layer)

                    bodies(sp, FT // 2, load_body)
                elif ph.name == "a_out":
                    a = ph.index // 3
                    load_unit(Unit(ph, 0))
                    load_unit(Unit(ph, 1))
                    for quad in range(2):
                        hs = heads_of(quad)
                        for d in range(2):
                            sp.wait_ge(dn_dve[d], N_DV * (6 * a + quad) + DV_STATE)
                            sp.dma_start(out["state"][a, d, hs].rearrange("h k v -> k h v"), state[:, d, hs]).then_inc(state_stored, 16)
                        sp.wait_ge(state_stored, 16 * (4 * a + 2 * quad + 2))
                        for d in range(2):
                            sp.dma_start(state[:, d, hs], inp["state_a"][a, d, hs].rearrange("h k v -> k h v")).then_inc(state_in, 16)
                    load_unit(Unit(ph, 2))
                elif ph.name == "a_in":
                    def load_pair(b, first, last):
                        for u in range(2):
                            load_unit(Unit(ph, u, 0 if first else b))
                    load_pair(0, True, False)
                    with sp.Fori(1, 4) as b:
                        load_pair(b, False, False)
                    for k in range(8, ph.units):
                        load_unit(Unit(ph, k))
                else:
                    for k in range(ph.units):
                        load_unit(Unit(ph, k))
        sp.wait_ge(stored, 16 * NT)

    @block.gpsimd
    def _(pool):
        steps = Steps(pool, pool_seq)
        stores = [0]
        pool.dma_start(cols[:], inp["cols"]).then_inc(consts_in, 16)
        pool.dma_start(ident[:], inp["ident"]).then_inc(consts_in, 16)
        for t in range(NT):
            src = inp["x_prompt"] if t == 0 else inp["x_sample"][(t - 1) * P:t * P]
            pool.dma_start(x[:, t], src).then_inc(x_in, 16)
        pool.dma_start(tri[:], inp["tri"]).then_inc(consts_in, 16)
        pool.dma_start(rope_tab[:], inp["rope_tab"]).then_inc(consts_in, 16)
        pool.dma_start(rows[:], inp["rows"].to_broadcast([P, ROWS])).then_inc(consts_in, 16)
        pool.memset(ones[:], 1.0)
        pool.memset(bias_eps[:], EPS)
        pool.memset(neg_half[:], -0.5).then_inc(pool_init, 1)
        pool.wait_ge(pool_init, 1)

        def root(n, width, mean_of, ready):
            steps.settle(pool.tensor_scalar(rstd[:, 0:width], sumsq[:, 0:width], 1.0 / mean_of, EPS, ALU.mult, ALU.add))
            pool.tensor_tensor(rstd[:, 0:width], rstd[:, 0:width], neg_half[:, 0:width], ALU.pow).then_inc(ready, 1)

        def norm_root(r):
            pool.wait_ge(sumsq_ready, 3 * r + 3)
            root(r, NT, D, rstd_ready)

        def residual(r):
            for t in range(NT):
                pool.wait_ge(res_prod, 6 * r + 2 * t + 1)
                pool.tensor_tensor(x[:, t, 0:512], x[:, t, 0:512], res_tmp[:, 2 * t % 3], ALU.add).then_inc(res_pool, 1)

        def mixer_root(layer):
            pool.wait_ge(oss_ready, 3 * (layer - (layer > 2)) + 3)
            root(0, 24, P, orstd_ready)

        def mixer_root(layer):
            i = tail_index(layer)
            pool.wait_ge(oss_ready, NT * i + NT)
            root(24, 24, P, orstd_ready)

        def pool_setup(r):
            pool.dma_start(inv_count[:].rearrange("p g t -> p (g t)"),
                           inp["inv_count"].to_broadcast([P, 4 * POOL_OUT])).then_inc(count_in, 16)
            pool.wait_ge(gate_mm, 4 * r + 4)
            pool.wait_ge(res_dve, NT * r)
            pool.memset(hpad[:], 0.0).then_inc(hpad_zero, 1)

        def attention(layer):
            pool.dma_start(past_k[:], inp["past_k"]).then_inc(past_in, 16)
            pool.dma_start(past_v[:], inp["past_v"]).then_inc(past_in, 16)
            pool.wait_ge(qkv_copied, 8 * NT)
            pool.dma_start(out["cache_k"], at_k[:, 0]).then_inc(cache_out, 16)
            pool.dma_start(out["cache_v"], at_v[:, 0]).then_inc(cache_out, 16)

        def ffn(f):
            pool.wait_ge(tr_ready, KT * (3 * (f // 2) + 2 * (f % 2)) + KT)

            def body(b, first, last):
                for _, m, slot, landed, layer in mod_steps(f, b, first, last):
                    mod_pool(pool, mod_raw[:, slot], mod_landed[slot], landed, m)
            bodies(pool, FT // 2, body)

        def delta_net(layer):
            a = layer // 3
            pool.wait_ge(*mod_count("dve", MOD_UNITS * (DEPTH if a else 1)))
            pool.dma_start(level_mask[:], inp["level_mask"]).then_inc(mask_in, 16)
            pool.wait_ge(mask_in, 16 * (a + 1))
            pool.wait_ge(xT_ready, xT_base(3 * layer + 1) + KT)
            pool.memset(scratch[:, 0:2], 0.0).then_inc(pad_zero, 1)
            pool.wait_ge(gc_done, a + 1)
            pool.memset(state[:], 0.0).then_inc(state_set, 1)
            pool.wait_ge(tok_v, KT * a + KT)
            pool.wait_ge(small_ready, a + 1)
            for pair, (chunks, quad) in enumerate(PAIRS):
                g = 6 * a + pair
                hs = heads_of(quad)
                for d in range(2):
                    w = work[d]
                    pool.wait_ge(dn_act[d], N_AC * g + AC_EXP)
                    pool.tensor_tensor(w[W_E][:], w[W_E][:], per_head(tri[:, d]), ALU.mult).then_inc(dn_pool[d], 1)
                for lev in range(LEVELS):
                    for d in range(2):
                        w = work[d]
                        if lev == 2:
                            beta = small(SM_BETA, chunks[d], d, quad)
                            pool.tensor_tensor(w[W_VB][:], dn_v[:, chunks[d], hs], beta, ALU.mult).then_inc(dn_pool[d], 1)
                        if lev == 0:
                            pool.wait_ge(dn_dve[d], N_DV * g + DV_A)
                        if lev >= 2:
                            pool.wait_ge(dn_mm[d], N_MM * g + mm_y(lev - 2))
                        pool.tensor_tensor(w[W_MASK + lev % 2][:], w[W_A][:], per_head(level_mask[:, d, lev]),
                                           ALU.mult).then_inc(dn_pool[d], 1)
                for d in range(2):
                    pool.wait_ge(dn_mm[d], N_MM * g + MM_QS)
                    pool.tensor_tensor(state[:, d, hs], state[:, d, hs], small(SM_GLAST, chunks[d], d, quad),
                                       ALU.mult).then_inc(dn_pool[d], 1)
                for d in range(2):
                    if not writes_first(pair, d):
                        pool.wait_ge(dn_dve[1 - d], N_DV * (g if pair < 2 else g - 2) + DV_O)
                        pool.wait_ge(dn_dve[d], N_DV * g + DV_O)
                        o = dn_o[:, chunks[d], hs]
                        pool.tensor_tensor(o, o, work[d][W_E][:], ALU.add).then_inc(dn_sum[d], 1)

        for m in range(MOD_PROLOGUE):
            if m == 0:
                pool.wait_ge(cond_ready, 1)
            mod_pool(pool, *mod_operand(m), m)
        for r in range(NORMS):
            kind = ("ffn", "abca"[r // 3], "ffn")[r % 3]
            norm_root(r)
            if kind == "ffn" and r < 3 * DEPTH - 1:
                ffn(2 * (r // 3) + r % 3 // 2)
            if kind == "c":
                pool_setup(r)
            if kind == "a":
                delta_net(r // 3)
                mixer_root(r // 3)
            if kind == "b":
                attention(r // 3)
                mixer_root(r // 3)
            residual(r)
        pool.wait_ge(gate_mm, 4 * NORMS)
        pool.dma_start(final_row[:], inp["final_g"].to_broadcast([P, D])).then_inc(count_in, 16)
        norm_root(NORMS)
        for t in range(NT):
            pool.wait_ge(y_ready, t + 1)
            dst = out["y_prompt"] if t == 0 else out["y_sample"][(t - 1) * P:t * P]
            pool.dma_start(dst, xhat[:, t]).then_inc(stored, 16)

    @block.scalar
    def _(act):
        steps = Steps(act, act_seq)

        def round_part(unit, q):
            if q >= unit.parts:
                return
            if q == 0:
                act.wait_ge(raw_landed[unit.slot], unit.landed)
            if not unit.first_two:
                which, count = release(unit, q)
                act.wait_ge(part_done[which], count)
            w = unit.width(q)
            act.activation(split_hi[:, unit.slot, q, 0:w], raw[:, unit.slot, q, 0:w], ACT.Copy).then_inc(hi_ready, 1)

        def round_unit(unit):
            for q in range(3):
                round_part(unit, q)

        act.wait_ge(cond_in, 16)
        act.activation(cond[:], cond[:], ACT.Silu).then_inc(cond_ready, 1)
        for m in range(MOD_PROLOGUE):
            mod_act(act, m, 0, m)
        act.wait_ge(*mod_count("dve", len(mod_first)))
        act.wait_ge(consts_in, 16 * CONSTS)
        round_unit(Unit(phases[0], 0))

        def norm(r, to_pad=False):
            act.wait_ge(*mod_count("act", mod_before(r)))
            for t in range(NT):
                if r == 0:
                    act.wait_ge(x_in, 16 * NT)
                else:
                    act.wait_ge(res_pool, NT * (r - 1) + t + 1)
                    act.wait_ge(res_dve, NT * (r - 1) + t + 1)
                act.activation(xhat[:, t], x[:, t], ACT.Square, accum_out=sumsq[:, t:t + 1]).then_inc(sumsq_ready, 1)
            if r == NORMS:
                return
            for i in range(4):
                act.wait_ge(gate_mm, 4 * r + i + 1)
                act.activation(gate_bc[:, i // 2, (i % 2) * 512:(i % 2) * 512 + 512], ps[i][:], ACT.Copy).then_inc(gate_ready, 1)
            par, v0 = vec_of(r)
            act.wait_ge(scale_ready, r + 1)
            for k in range(KT):
                act.wait_ge(tr_ready, KT * r + k + 1)
                if k >= 4 and not to_pad:
                    act.wait_ge(xT_ready, xT_base(r) + k - 3)
                if k == 0 and to_pad:
                    act.wait_ge(hpad_zero, 1)
                for c, (lo, hi) in enumerate(CHANNEL_SPANS):
                    pad = POOL_PAD * (c + 1)
                    dst = hpad[:, k, lo + pad:hi + pad] if to_pad else scratch[:, k % 4, lo:hi]
                    ins = act.activation(dst, ps[NORM_BANK[k]][:, lo:hi], ACT.Identity,
                                         bias=modv[:, par, v0 + k, c:c + 1], scale=scale_col[:, k, c:c + 1])
                ins.then_inc(hpad_ready if to_pad else xn_ready, 1)

        def ffn(ph):
            f = ph.index
            s0 = FT * f

            def body(b, first, last):
                for u in range(2):
                    k = u if first else ph.units - 2 + u if last else u
                    unit = Unit(ph, k, 0 if first or last else b)
                    nxt = following(unit) if (last and u == 1) else Unit(ph, k + 1, 0 if first or last else b)
                    j = unit.local
                    par = u % 2
                    if nxt:
                        round_part(nxt, 0)
                        round_part(nxt, 1)
                    act.wait_ge(part_done[0], done(unit, 0))
                    if not (first and f == 0):
                        act.wait_ge(prod_done, s0 + j - 1)
                    act.activation(silu_g[:, par], ps[BANK_GATE][:, 0:T], ACT.Silu).then_inc(silu_done, 1)
                    act.wait_ge(prod_done, s0 + j + 1)
                    if not (first):
                        act.wait_ge(part_done[2], done(unit, 2) - 2)
                    act.activation(hid_hi[:, par], hidden[:, par], ACT.Copy).then_inc(hid_hi_done, 1)
                    if nxt:
                        round_part(nxt, 2)
                    for step, m, _, _, layer in mod_steps(f, b, first, last):
                        if step == u:
                            mod_act(act, m, layer, m - MOD_UNITS * layer)

            bodies(act, FT // 2, body)

        def proj_a(ph):
            a = ph.index // 3

            def copy_padded(i, w, unit, q):
                act.wait_ge(part_done[q], done(unit, q))
                if not (isinstance(i, int) and i < 2):
                    act.wait_ge(conv_step, CONV * (24 * a + i - 1))
                for c, (lo, hi) in enumerate(CHANNEL_SPANS):
                    pad = CONV_PAD * (c + 1)
                    ins = act.activation(scratch[:, w % 2, lo + pad:hi + pad], ps[PROJ_BANK[w % 3]][:, lo:hi], ACT.Copy)
                ins.then_inc(tile_used, 1)

            def silu(i, w):
                act.wait_ge(conv_step, CONV * (24 * a + i + 1))
                for c, (lo, hi) in enumerate(CHANNEL_SPANS):
                    pad = 2 * CONV_PAD * c // 2
                    dst = qkvz[:, bass.ds(i, 1), lo:hi].rearrange("p o c -> p (o c)")
                    ins = act.activation(dst, scratch[:, 2 + w % 2, lo + pad:hi + pad], ACT.Silu)
                ins.then_inc(conv_silu, 1)

            def body(b, first):
                for u in range(2):
                    unit = Unit(ph, u, 0 if first else b)
                    nxt = Unit(ph, u + 1, 0 if first else b)
                    for q in range(3):
                        w = 3 * u + q
                        i = w if first else 6 * b + w
                        round_part(nxt, q)
                        copy_padded(i, w, unit, q)
                        if not (first and w == 0):
                            silu(i - 1, w + 1)

            act.wait_ge(pad_zero, a + 1)
            body(0, True)
            with act.Fori(1, 4) as b:
                body(b, False)
            silu(23, 1)
            for k in range(8, ph.units):
                unit = Unit(ph, k)
                nxt = Unit(ph, k + 1) if k + 1 < ph.units else None
                for q in range(3):
                    i = 3 * k + q
                    if nxt:
                        round_part(nxt, q)
                    if i >= 4 * HEADS:
                        continue
                    act.wait_ge(part_done[q], done(unit, q))
                    act.activation(qkvz[:, i], ps[PROJ_BANK[i % 3]][:, 0:T], ACT.Copy).then_inc(tile_used, 1)
                    for e in (2 * (i - 24), 2 * (i - 24) + 1):
                        act.wait_ge(ss_done, 16 * a + e + 1)
                        if e >= 2:
                            act.wait_ge(unit_ready, 16 * a + e - 1)
                        row = scratch[:, 2 + e % 2, 0:T]
                        steps.settle(act.activation(row, ps[e % 2][:, 0:T], ACT.Ln, bias=bias_eps[:, 0:1]))
                        act.activation(row, row, ACT.Exp, scale=-0.5).then_inc(r_ready, 1)
            act.wait_ge(ab_in, a + 1)
            flat = lambda i: dn_small[:, i].rearrange("p c d h -> p (c d h)")
            steps.settle(act.activation(flat(SM_ABS), flat(SM_ABS), ACT.Exp, scale=-1.0))
            act.activation(flat(SM_B), flat(SM_B), ACT.Exp, scale=-1.0)
            act.activation(at_small[:, 0:16], rows[:, ROW_A_LOG + 16 * a:ROW_A_LOG + 16 * a + 16], ACT.Exp)
            act.activation(flat(SM_ABS), flat(SM_ABS), ACT.Ln, bias=ones[:, 0:1]).then_inc(ab_exp, 1)
            for h in range(HEADS):
                act.wait_ge(tokT_done, 16 * a + h + 1)
                act.activation(dn_v[:, :, h], ps[2 + h % 2][:, 0:T].rearrange("p (c e) -> p c e", c=NT), ACT.Copy).then_inc(tok_v, 1)
            act.wait_ge(decay_in, a + 1)
            act.activation(flat(SM_EG), flat(SM_GC), ACT.Exp)
            act.activation(flat(SM_GLAST), flat(SM_TOTAL), ACT.Exp)
            act.activation(flat(SM_EKD), flat(SM_EKD), ACT.Exp).then_inc(decay_out, 1)

        def delta_net(layer):
            a = layer // 3
            for pair in range(len(PAIRS)):
                g = 6 * a + pair
                for d in range(2):
                    e = work[d][W_E]
                    act.wait_ge(dn_dve[d], N_DV * g + DV_MIN)
                    act.activation(e[:], e[:], ACT.Exp).then_inc(dn_act[d], 1)
                for lev in range(LEVELS):
                    for d in range(2):
                        act.wait_ge(dn_mm[d], N_MM * g + mm_u(lev))
                        act.activation(work[d][W_U][:].rearrange("p h c -> p (h c)"), ps[4 * d + 2][:], ACT.Copy).then_inc(dn_act[d], 1)
                for d in range(2):
                    act.wait_ge(dn_mm[d], N_MM * g + MM_VN)
                    act.activation(work[d][W_VN][:].rearrange("p h c -> p (h c)"), ps[4 * d][:], ACT.Copy).then_inc(dn_act[d], 1)
            act.activation(qkvz[:, 24:32].rearrange("p h t -> p (h t)"), qkvz[:, 24:32].rearrange("p h t -> p (h t)"),
                           ACT.Silu).then_inc(z_ready, 1)
            for d in range(2):
                act.wait_ge(dn_dve[d], N_DV * (6 * a + 6))
                act.wait_ge(dn_sum[d], (4 if d else 2) * (a + 1))

        def tail(layer, kind, out_ph):
            m = tail_index(layer)
            round_unit(Unit(out_ph, 0))
            round_unit(Unit(out_ph, 1))
            o = dn_o if kind == "a" else at_o
            for t in range(NT):
                act.activation(sq_tmp[:, t], o[:, t], ACT.Square).then_inc(osq_ready, 1)
            for h in range(HEADS):
                row = scratch[:, h % 4, 0:T]
                if kind == "a":
                    act.wait_ge(on_ready, HEADS * layer + h + 1)
                else:
                    act.wait_ge(otr_ready, HEADS * m + h + 1)
                    if h >= 4:
                        act.wait_ge(oT_ready, oT_base(layer) + h - 3)
                    act.activation(row, ps[6 + h % 2][:, 0:T], ACT.Copy, scale=at_small[:, AT_NORM:AT_NORM + 1]).then_inc(on_ready, 1)
                    act.wait_ge(on_ready, HEADS * layer + h + 1)
                act.activation(xT_hi[:, h], row, ACT.Copy).then_inc(ohi_ready, 1)
                if h == 5:
                    round_unit(Unit(out_ph, 2))
            nxt = following(Unit(out_ph, out_ph.units - 1))
            if nxt:
                round_unit(nxt)

        def attention(ph):
            act.wait_ge(lam_ready, 1)
            lam = at_small[:, AT_LAM:AT_LAM + 2]
            act.activation(lam, lam, ACT.Exp).then_inc(lam_exp, 1)
            dests = (at_q, at_k, at_v)
            for k in range(ph.units):
                unit = Unit(ph, k)
                for t in range(NT):
                    if k + 1 < ph.units:
                        round_part(Unit(ph, k + 1), t)
                    act.wait_ge(part_done[t], done(unit, t))
                    lo, end = 3 * P * k, 3 * P * (k + 1)
                    start = lo
                    while start < end:
                        stop = min(end, (start // D + 1) * D)
                        ins = act.activation(dests[start // D][:, t, start % D:start % D + stop - start],
                                             ps[PROJ_BANK[t]][:, start - lo:stop - lo], ACT.Copy)
                        start = stop
                    ins.then_inc(qkv_copied, 1)
            for h in range(HEADS):
                act.wait_ge(head_tr, 2 * h + 1)
                act.activation(qT[:, h], ps[h % 2][:, 0:T], ACT.Copy, scale=DH ** -0.5).then_inc(q_head, 1)
            items = NT * HEADS
            for i in range(items + 1):
                if i < items:
                    par, keys = i % 2, P if i % NT == 0 else T
                    act.wait_ge(max_done, i + 1)
                    if i >= 2:
                        act.wait_ge(pT_done, i - 1)
                    for c in range(2):
                        m = at_small[:, AT_NEG_MAX + 2 * par + c:AT_NEG_MAX + 2 * par + c + 1]
                        total = at_small[:, AT_SUM + 2 * par + c:AT_SUM + 2 * par + c + 1]
                        ins = act.activation(prob[:, par, c, 0:keys], ps[4 * par + c][:, 0:keys], ACT.Exp, bias=m, accum_out=total)
                    ins.then_inc(exp_done, 1)
                if i >= 1:
                    j = i - 1
                    par, keys = j % 2, P if j % NT == 0 else T
                    act.wait_ge(pT_done, j + 1)
                    if j >= 2:
                        act.wait_ge(ao_done, j - 1)
                    act.activation(probT[:, par, 0:keys], ps[4 * par + 2][:, 0:keys], ACT.Copy).then_inc(pT_copied, 1)
            act.wait_ge(ao_done, items)
            act.wait_ge(ao_copied, items)
            act.wait_ge(prob_done, items)
            act.wait_ge(cache_out, 32)

        def pooling(ph):
            round_unit(following(Unit(ph, 0)))
            layer = ph.index
            for k in range(KT):
                act.wait_ge(on_ready, KT * layer + k + 1)
                act.activation(xT_hi[:, k], scratch[:, k % 4, 0:T], ACT.Copy).then_inc(ohi_ready, 1)


        for r in range(NORMS):
            phs = by_stage[r]
            kind = phs[0].name[0]
            norm(r, to_pad=kind == "c")
            if kind == "f":
                ffn(phs[0])
            if kind == "a":
                proj_a(phs[0])
                delta_net(r // 3)
                tail(r // 3, "a", phs[1])
            if kind == "b":
                attention(phs[0])
                tail(r // 3, "b", phs[1])
            if kind == "c":
                pooling(phs[0])
        norm(NORMS)

    @block.vector
    def _(dve):
        steps = Steps(dve, dve_seq)

        def rest_part(unit, q):
            if q >= unit.parts:
                return
            w = unit.width(q)
            dve.wait_ge(hi_ready, unit.split_count(q))
            dve.tensor_tensor(split_lo[:, unit.slot, q, 0:w], raw[:, unit.slot, q, 0:w],
                              f32(split_hi[:, unit.slot, q, 0:w]), ALU.subtract).then_inc(lo_ready, 1)

        def rest_unit(unit):
            for q in range(3):
                rest_part(unit, q)

        def vectors(r):
            par, v0 = vec_of(r)
            dve.wait_ge(*mod_count("dve", mod_needed(r)))
            dve.wait_ge(*mod_count("act", mod_needed(r)))
            v = modv[:, par, v0:v0 + 3 * KT]
            b0 = COL_MOD_B + N_MOD * KT * (r // 3) + v0
            b = cols[:, b0:b0 + 3 * KT].rearrange("p (k o) -> p k o", o=1).to_broadcast([P, 3 * KT, 2])
            steps.settle(dve.tensor_tensor(v, v, b, ALU.add))

        def gates(r):
            vectors(r)
            par, v0 = vec_of(r)
            gate = modv[:, par, v0 + 2 * KT:v0 + 3 * KT]
            if r % 3 != 1:
                steps.settle(dve.tensor_scalar(gate_col[:], gate, 0.5, None, ALU.mult))
            elif r == 7:
                cs = cols[:, COL_C_SCALE:COL_C_SCALE + KT].rearrange("p (k o) -> p k o", o=1).to_broadcast([P, KT, 2])
                steps.settle(dve.tensor_tensor(gate_col[:], gate, cs, ALU.mult))
            else:
                steps.settle(dve.tensor_copy(gate_col[:], gate))
            if r:
                dve.wait_ge(gate_mm, 4 * r)
            for c in range(2):
                i = ident[:].rearrange("p (o c) -> p o c", o=1).to_broadcast([P, KT, P])
                dve.tensor_tensor(diag[:, c], i, gate_col[:, :, c:c + 1].to_broadcast([P, KT, P]),
                                  ALU.mult).then_inc(diag_ready, 1)

        def scales(r):
            par, v0 = vec_of(r)
            steps.settle(dve.tensor_scalar(scale_col[:], modv[:, par, v0 + KT:v0 + 2 * KT], 1.0, None, ALU.add))
            g = cols[:, COL_NORM_G + KT * r:COL_NORM_G + KT * (r + 1)].rearrange("p (k o) -> p k o", o=1)
            dve.tensor_tensor(scale_col[:], scale_col[:], g.to_broadcast([P, KT, 2]), ALU.mult).then_inc(scale_ready, 1)

        def norm(r, to_pad=False):
            dve.wait_ge(rstd_ready, r + 1)
            for t in range(NT):
                dve.tensor_scalar(xhat[:, t], x[:, t], rstd[:, t:t + 1], None, ALU.mult).then_inc(xhat_ready, 1)
            if to_pad:
                return
            for k in range(KT):
                dve.wait_ge(xn_ready, xT_base(r) + k + 1)
                row = scratch[:, k % 4, 0:T]
                steps.settle(dve.tensor_copy(xT_hi[:, k], row))
                dve.tensor_tensor(xT_lo[:, k], row, f32(xT_hi[:, k]), ALU.subtract).then_inc(xT_ready, 1)

        def ffn(ph):
            f = ph.index
            s0 = FT * f

            def body(b, first, last):
                for u in range(2):
                    k = u if first else ph.units - 2 + u if last else u
                    body_of = 0 if first or last else b
                    unit = Unit(ph, k, body_of)
                    nxt = following(unit) if (last and u == 1) else Unit(ph, k + 1, body_of)
                    j = unit.local
                    par = u % 2
                    if nxt:
                        rest_part(nxt, 0)
                        rest_part(nxt, 1)
                    dve.wait_ge(part_done[1], done(unit, 1))
                    dve.wait_ge(silu_done, s0 + j + 1)
                    dve.tensor_tensor(hidden[:, par], silu_g[:, par], ps[BANK_UP][:, 0:T], ALU.mult).then_inc(prod_done, 1)
                    dve.wait_ge(hid_hi_done, s0 + j + 1)
                    dve.tensor_tensor(hid_lo[:, par], hidden[:, par], f32(hid_hi[:, par]), ALU.subtract).then_inc(hid_done, 1)
                    if nxt:
                        rest_part(nxt, 2)
                    for step, m, slot, landed, layer in mod_steps(f, b, first, last):
                        if step == u:
                            mod_dve(dve, mod_raw[:, slot], mod_landed[slot], landed, m, layer, m - MOD_UNITS * layer)

            bodies(dve, FT // 2, body)

        def residual(r, last_unit):
            for q in range(3):
                dve.wait_ge(part_done[q], done(last_unit, q)) if q < last_unit.parts else None
            dve.wait_ge(gate_ready, 4 * r + 4)
            for i in range(2 * NT):
                t, half = divmod(i, 2)
                span = slice(512 * half, 512 * half + 512)
                if i >= 3:
                    if (i - 3) % 2 == 0:
                        dve.wait_ge(res_pool, NT * r + (i - 3) // 2 + 1)
                    else:
                        dve.wait_ge(res_dve, NT * r + (i - 3) // 2 + 1)
                dve.tensor_tensor(res_tmp[:, i % 3], ps[i][:], gate_bc[:, min(t, 1), span], ALU.mult).then_inc(res_prod, 1)
                if half:
                    dve.wait_ge(res_prod, 6 * r + i + 1)
                    dve.tensor_tensor(x[:, t, span], x[:, t, span], res_tmp[:, i % 3], ALU.add).then_inc(res_dve, 1)

        def proj_a(ph):
            a = ph.index // 3

            def convolve(i, w):
                dve.wait_ge(tile_used, 32 * a + i + 1)
                if not (isinstance(i, int) and i < 2):
                    dve.wait_ge(conv_silu, 24 * a + i - 1)
                elif a:
                    dve.wait_ge(conv_silu, 24)
                src, dst = scratch[:, w % 2], scratch[:, 2 + w % 2, 0:CONV_OUT]
                for tap in range(CONV):
                    weight = cols[:, bass.ds(COL_CONV + 24 * CONV * a + CONV * i + tap, 1)]
                    if tap == 0:
                        ins = dve.tensor_scalar(dst, src[:, 0:CONV_OUT], weight, None, ALU.mult)
                    else:
                        dve.wait_ge(conv_step, CONV * (24 * a + i) + tap)
                        ins = dve.scalar_tensor_tensor(dst, src[:, tap:tap + CONV_OUT], weight, dst, ALU.mult, ALU.add)
                    ins.then_inc(conv_step, 1)

            def body(b, first):
                for u in range(2):
                    nxt = Unit(ph, u + 1, 0 if first else b)
                    for q in range(3):
                        w = 3 * u + q
                        rest_part(nxt, q)
                        convolve(w if first else 6 * b + w, w)

            body(0, True)
            with dve.Fori(1, 4) as b:
                body(b, False)

            def square(e):
                dve.wait_ge(conv_silu, 24 * a + (24 if e < 2 else e + 1))
                if e >= 2:
                    dve.wait_ge(ss_done, 16 * a + e - 1)
                dve.tensor_tensor(scratch[:, e % 2, 0:T], qkvz[:, e], qkvz[:, e], ALU.mult).then_inc(sq_ready, 1)

            def scale_unit(e):
                dve.wait_ge(r_ready, 16 * a + e + 1)
                row = scratch[:, 2 + e % 2, 0:T]
                if e < HEADS:
                    ins = dve.scalar_tensor_tensor(qkvz[:, e], qkvz[:, e], P ** -0.5, row, ALU.mult, ALU.mult)
                else:
                    ins = dve.tensor_tensor(qkvz[:, e], qkvz[:, e], row, ALU.mult)
                ins.then_inc(unit_ready, 1)

            square(0)
            square(1)
            for k in range(8, ph.units):
                nxt = Unit(ph, k + 1) if k + 1 < ph.units else None
                for q in range(3):
                    if nxt:
                        rest_part(nxt, q)
                    z = 3 * k + q - 24
                    if z < HEADS:
                        for e in (2 * z, 2 * z + 1):
                            scale_unit(e)
                            if e + 2 < 16:
                                square(e + 2)
            flat = lambda i: dn_small[:, i].rearrange("p c d h -> p (c d h)")
            by_c = lambda i: dn_small[:, i].rearrange("p c d h -> p c (d h)")
            last = Unit(ph, ph.units - 1)
            dve.wait_ge(part_done[2], done(last, 2))
            ab = ps[4][:, 0:NT * AB].rearrange("p (c d s h) -> p c d s h", c=NT, d=2, s=2)
            for c in range(NT):
                dt = rows[:, ROW_DT + 16 * a:ROW_DT + 16 * a + 16].rearrange("p (d h) -> p d h", d=2)
                ins = dve.tensor_tensor(dn_small[:, SM_X, c], ab[:, c, :, 0], dt, ALU.add)
                steps.settle(dve.tensor_copy(dn_small[:, SM_B, c], ab[:, c, :, 1]))
            dve.scalar_tensor_tensor(flat(SM_ABS), flat(SM_X), -1.0, flat(SM_X), ALU.mult, ALU.max).then_inc(ab_in, 1)
            dve.wait_ge(ab_exp, a + 1)
            steps.settle(dve.scalar_tensor_tensor(flat(SM_X), flat(SM_X), 0.0, flat(SM_ABS), ALU.max, ALU.add))
            na = at_small[:, 0:16].rearrange("p (o c) -> p o c", o=1).to_broadcast([P, NT, 16])
            dve.scalar_tensor_tensor(by_c(SM_G), by_c(SM_X), -1.0, na, ALU.mult, ALU.mult).then_inc(g_ready, 1)
            steps.settle(dve.tensor_scalar(flat(SM_B), flat(SM_B), 1.0, None, ALU.add))
            steps.settle(dve.reciprocal(flat(SM_BETA), flat(SM_B)))
            dve.wait_ge(gc_done, a + 1)
            both = dn_small[:, SM_GC:SM_TOTAL + 1].rearrange("p i c d h -> p (i c d h)")
            steps.settle(dve.tensor_copy(both, ps[4][:, 0:4 * NT * HEADS]))
            dve.tensor_tensor(flat(SM_EKD), flat(SM_TOTAL), flat(SM_GC), ALU.subtract).then_inc(decay_in, 1)
            dve.wait_ge(decay_out, a + 1)
            dve.tensor_tensor(flat(SM_BEG), flat(SM_BETA), flat(SM_EG), ALU.mult).then_inc(small_ready, 1)
            dve.wait_ge(small_ready, a + 1)
            for h in range(HEADS):
                dve.wait_ge(tokT_done, 16 * a + HEADS + h + 1)
                dve.tensor_copy(dn_k[:, :, h], ps[2 + h % 2][:, 0:T].rearrange("p (c e) -> p c e", c=NT)).then_inc(tok_k, 1)

        def delta_net(layer):
            a = layer // 3

            def bank(d, i):
                return ps[4 * d + i][:].rearrange("p (h c) -> p h c", h=GROUP)

            def on(d, ins):
                ins.then_inc(dn_dve[d], 1)

            for pair, (chunks, quad) in enumerate(PAIRS):
                g = 6 * a + pair
                hs = heads_of(quad)
                mm = lambda d, n: dve.wait_ge(dn_mm[d], N_MM * g + n)
                own = lambda d, n: dve.wait_ge(dn_dve[d], N_DV * g + n)
                val = lambda which, d: small(which, chunks[d], d, quad)
                for d in range(2):
                    on(d, dve.tensor_tensor(work[d][W_Y][:], per_head(tri[:, d]), val(SM_G, d), ALU.mult))
                for d in range(2):
                    e = work[d][W_E][:]
                    sums = writes_first(pair - 1, d) if pair else True
                    if not sums:
                        dve.wait_ge(dn_sum[d], sum_count(a, pair - 1, d))
                    mm(d, MM_D)
                    on(d, dve.tensor_tensor(e, bank(d, 2), val(SM_GC, d), ALU.subtract))
                    own(d, DV_ARG)
                    on(d, dve.tensor_scalar(e, e, 0.0, None, ALU.min))
                for d in range(2):
                    w = work[d]
                    mm(d, MM_KQ)
                    dve.wait_ge(dn_pool[d], N_PO * g + PO_E)
                    on(d, dve.tensor_tensor(w[W_A][:], bank(d, 0), w[W_E][:], ALU.mult))
                    on(d, dve.tensor_tensor(w[W_ATT][:], bank(d, 1), w[W_E][:], ALU.mult))
                for lev in range(LEVELS):
                    for d in range(2):
                        mm(d, mm_y(lev))
                        on(d, dve.tensor_tensor(work[d][W_Y][:], bank(d, 0), val(SM_BETA, d), ALU.mult))
                    for d in range(2):
                        w = work[d]
                        if lev == 0:
                            own(d, dv_y(0))
                            on(d, dve.tensor_tensor(w[W_T][:], per_head(ident[:]), w[W_Y][:], ALU.subtract))
                        else:
                            mm(d, mm_z(lev))
                            on(d, dve.tensor_tensor(w[W_T][:], w[W_T][:], bank(d, 1), ALU.subtract))
                for d in range(2):
                    w = work[d]
                    mm(d, MM_KS)
                    on(d, dve.tensor_tensor(w[W_E][:], bank(d, 3), val(SM_BEG, d), ALU.mult))
                    dve.wait_ge(dn_pool[d], N_PO * g + PO_VB)
                    own(d, DV_KS)
                    on(d, dve.tensor_tensor(w[W_VB][:], w[W_VB][:], w[W_E][:], ALU.subtract))
                for d in range(2):
                    w = work[d]
                    mm(d, MM_QS)
                    own(d, DV_R)
                    on(d, dve.tensor_tensor(w[W_E][:], bank(d, 2), val(SM_EG, d), ALU.mult))
                    mm(d, MM_VN)
                    dve.wait_ge(dn_act[d], N_AC * g + AC_VN)
                    on(d, dve.tensor_tensor(w[W_T][:], bank(d, 0), val(SM_EKD, d), ALU.mult))
                for d in range(2):
                    w = work[d]
                    mm(d, MM_OI)
                    own(d, DV_VS)
                    dst = dn_o[:, chunks[d], hs] if writes_first(pair, d) else w[W_E][:]
                    on(d, dve.tensor_tensor(dst, w[W_E][:], bank(d, 1), ALU.add))
                for d in range(2):
                    mm(d, MM_DS)
                    dve.wait_ge(dn_pool[d], N_PO * g + PO_STATE)
                    on(d, dve.tensor_tensor(state[:, d, hs], state[:, d, hs], bank(d, 3), ALU.add))

        def sum_count(a, pair, d):
            per = [int(not writes_first(i, d)) for i in range(len(PAIRS))]
            return sum(per) * a + sum(per[:pair + 1])

        def tail(layer, kind, out_ph):
            m = tail_index(layer)
            rest_unit(Unit(out_ph, 0))
            rest_unit(Unit(out_ph, 1))
            o = dn_o if kind == "a" else at_o
            for t in range(NT):
                dve.wait_ge(osq_ready, NT * m + t + 1)
                dve.tensor_reduce(sumsq[:, HEADS * t:HEADS * t + HEADS], sq_tmp[:, t], AX.X, ALU.add).then_inc(oss_ready, 1)
            dve.wait_ge(orstd_ready, m + 1)
            for t in range(NT):
                r = rstd[:, HEADS * t:HEADS * t + HEADS].rearrange("p (h o) -> p h o", o=1).to_broadcast([P, HEADS, P])
                dve.tensor_tensor(o[:, t], o[:, t], r, ALU.mult).then_inc(ohat_ready, 1)
            for h in range(HEADS):
                row = scratch[:, h % 4, 0:T]
                if kind == "a":
                    if h == 0:
                        dve.wait_ge(z_ready, layer // 3 + 1)
                    dve.wait_ge(otr_ready, HEADS * m + h + 1)
                    dve.scalar_tensor_tensor(row, ps[6 + h % 2][:, 0:T], cols[:, COL_A_NORM + layer // 3:COL_A_NORM + layer // 3 + 1],
                                             qkvz[:, 24 + h], ALU.mult, ALU.mult).then_inc(on_ready, 1)
                dve.wait_ge(ohi_ready, HEADS * layer + h + 1)
                dve.tensor_tensor(xT_lo[:, h], row, f32(xT_hi[:, h]), ALU.subtract).then_inc(oT_ready, 1)
                if h == 5:
                    rest_unit(Unit(out_ph, 2))
            nxt = following(Unit(out_ph, out_ph.units - 1))
            if nxt:
                rest_unit(nxt)

        def attention(ph):
            lam_rows = rows[:, ROW_LAM:ROW_LAM + 4 * DH].rearrange("p (a b c) -> p a b c", a=2, b=2)
            steps.settle(dve.tensor_tensor(lam_prod[:], lam_rows[:, :, 0], lam_rows[:, :, 1], ALU.mult))
            dve.tensor_reduce(at_small[:, AT_LAM:AT_LAM + 2], lam_prod[:], AX.X, ALU.add).then_inc(lam_ready, 1)
            dve.wait_ge(lam_exp, 1)
            neg_lam = at_small[:, AT_NEG_LAM:AT_NEG_LAM + 1]
            steps.settle(dve.tensor_tensor(neg_lam, at_small[:, AT_LAM + 1:AT_LAM + 2], at_small[:, AT_LAM:AT_LAM + 1], ALU.subtract))
            steps.settle(dve.tensor_scalar(neg_lam, neg_lam, -LAM_INIT, None, ALU.add))
            steps.settle(dve.tensor_scalar(at_small[:, AT_NORM:AT_NORM + 1], cols[:, COL_B_NORM:COL_B_NORM + 1],
                                           1.0 - LAM_INIT, None, ALU.mult))
            for k in range(ph.units):
                if k + 1 < ph.units:
                    rest_unit(Unit(ph, k + 1))
                if k == 5:
                    rotate()
            for h in range(HEADS):
                dve.wait_ge(head_tr, 2 * h + 2)
                dve.tensor_copy(kT[:, h], ps[2 + h % 2][:]).then_inc(k_head, 1)
            items = NT * HEADS
            for i in range(items + 2):
                if i < items:
                    par, keys = i % 2, P if i % NT == 0 else T
                    dve.wait_ge(score_done, i + 1)
                    for c in range(2):
                        m = at_small[:, AT_NEG_MAX + 2 * par + c:AT_NEG_MAX + 2 * par + c + 1]
                        ins = dve.tensor_reduce(m, ps[4 * par + c][:, 0:keys], AX.X, ALU.max, negate=True)
                    ins.then_inc(max_done, 1)
                if 1 <= i <= items:
                    j = i - 1
                    par, keys = j % 2, P if j % NT == 0 else T
                    dve.wait_ge(exp_done, j + 1)
                    recip = at_small[:, AT_RECIP + 2 * par:AT_RECIP + 2 * par + 2]
                    second = at_small[:, AT_SCALED + par:AT_SCALED + par + 1]
                    steps.settle(dve.reciprocal(recip, at_small[:, AT_SUM + 2 * par:AT_SUM + 2 * par + 2]))
                    dve.tensor_scalar(second, recip[:, 1:2], neg_lam, None, ALU.mult)
                    p0, p1 = prob[:, par, 0, 0:keys], prob[:, par, 1, 0:keys]
                    steps.settle(dve.tensor_scalar(p0, p0, recip[:, 0:1], None, ALU.mult))
                    dve.scalar_tensor_tensor(p0, p1, second, p0, ALU.mult, ALU.add).then_inc(prob_done, 1)
                if i >= 2:
                    j = i - 2
                    dve.wait_ge(ao_done, j + 1)
                    dve.tensor_copy(at_o[:, j % NT, j // NT], ps[4 * (j % 2) + 3][:, 0:P]).then_inc(ao_copied, 1)

        def rotate():
            dve.wait_ge(qkv_copied, 6 * NT)
            groups = D // DH
            for t in range(1, NT):
                cos = rope_tab[:, t - 1, 0:1].to_broadcast([P, groups, DH])
                sin = rope_tab[:, t - 1, 1].rearrange("p (o b i f) -> p o b i f", o=1, b=2, i=2)
                for v in (at_q, at_k):
                    x3 = v[:, t].rearrange("p (g c) -> p g c", g=groups)
                    x4 = v[:, t].rearrange("p (g b i f) -> p g b i f", b=2, i=2, f=DH // 4)
                    r4 = rope_b[:].rearrange("p (g b i f) -> p g b i f", b=2, i=2, f=DH // 4)
                    dve.tensor_tensor(rope_a[:].rearrange("p (g c) -> p g c", g=groups), x3, cos, ALU.mult)
                    for i in range(2):
                        s4 = sin[:, :, :, i].to_broadcast([P, groups, 2, DH // 4])
                        ins = dve.tensor_tensor(r4[:, :, :, i], x4[:, :, :, 1 - i], s4, ALU.mult)
                    steps.settle(ins)
                    dve.tensor_tensor(v[:, t], rope_a[:], rope_b[:], ALU.add).then_inc(roped, 1)
                    dve.wait_ge(roped, 2 * (t - 1) + (1 if v is at_q else 2))

        def pooling(ph):
            layer = ph.index
            rest_unit(following(Unit(ph, 0)))
            dve.wait_ge(count_in, 16)

            def rest(k):
                dve.wait_ge(ohi_ready, KT * layer + k + 1)
                dve.tensor_tensor(xT_lo[:, k], scratch[:, k % 4, 0:T], f32(xT_hi[:, k]), ALU.subtract).then_inc(oT_ready, 1)

            for k in range(KT):
                dve.wait_ge(hpad_ready, k + 1)
                a, b = pool_tmp[:, 0], pool_tmp[:, 1]
                steps.settle(dve.tensor_tensor(a[:, 1:POOL_W], hpad[:, k, 0:POOL_W - 1], hpad[:, k, 1:POOL_W], ALU.add))
                reach = 1
                for _ in range(k // 2):
                    lo, hi = 2 * reach, POOL_W - 2 * reach
                    steps.settle(dve.tensor_tensor(b[:, lo:hi], a[:, lo - reach:hi - reach], a[:, lo + reach:hi + reach], ALU.add))
                    a, b = b, a
                    reach *= 2
                mean = pool_tmp[:, 2, 0:POOL_OUT]
                steps.settle(dve.tensor_tensor(mean, a[:, POOL_PAD:POOL_PAD + POOL_OUT], inv_count[:, k // 2], ALU.mult))
                for c, (lo, hi) in enumerate(CHANNEL_SPANS):
                    gap = POOL_PAD * c
                    ins = dve.tensor_tensor(scratch[:, k % 4, lo:hi], mean[:, lo + gap:hi + gap],
                                            hpad[:, k, lo + gap + POOL_PAD:hi + gap + POOL_PAD], ALU.subtract)
                ins.then_inc(on_ready, 1)
                if k:
                    rest(k - 1)
            rest(KT - 1)


        for m in range(MOD_PROLOGUE):
            if m == 0:
                dve.wait_ge(cond_ready, 1)
            mod_dve(dve, *mod_operand(m), m, 0, m)
            if m == MOD_PROLOGUE - 1:
                rest_unit(Unit(phases[0], 0))
        dve.wait_ge(consts_in, 16 * CONSTS)
        gates(0)
        for r in range(NORMS):
            phs = by_stage[r]
            kind = phs[0].name[0]
            scales(r)
            norm(r, to_pad=kind == "c")
            if kind == "f":
                ffn(phs[0])
            if kind == "a":
                proj_a(phs[0])
                delta_net(r // 3)
                tail(r // 3, "a", phs[1])
            if kind == "b":
                attention(phs[0])
                tail(r // 3, "b", phs[1])
            if kind == "c":
                pooling(phs[0])
            if r + 1 < NORMS:
                gates(r + 1)
            residual(r, Unit(phs[-1], phs[-1].units - 1))
        dve.wait_ge(rstd_ready, NORMS + 1)
        dve.wait_ge(count_in, 16 * (stages > 7) + 16)
        for t in range(NT):
            steps.settle(dve.tensor_scalar(xhat[:, t], x[:, t], rstd[:, t:t + 1], None, ALU.mult))
            dve.tensor_tensor(xhat[:, t], xhat[:, t], final_row[:], ALU.mult).then_inc(y_ready, 1)

    @block.tensor
    def _(pe):
        def three(out, w_hi, w_lo, a_hi, a_lo, start, stop, weights_stationary=True):
            pairs = ((w_hi, a_hi), (w_hi, a_lo), (w_lo, a_hi))
            for i, (w, a) in enumerate(pairs if weights_stationary else ((w_hi, a_hi), (w_lo, a_hi), (w_hi, a_lo))):
                lhsT, rhs = (w, a) if weights_stationary else (a, w)
                ins = pe.matmul(out, lhsT, rhs, start=start and i == 0, stop=stop and i == 2)
            return ins

        def norm(r):
            pe.wait_ge(diag_ready, 2 * r + 2)
            if r:
                pe.wait_ge(res_prod, 6 * r)
            for i in range(4):
                d = diag[:, i // 2].rearrange("p k c -> p (k c)")
                pe.matmul(ps[i][:], ones[:], d[:, (i % 2) * 512:(i % 2) * 512 + 512], start=True, stop=True).then_inc(gate_mm, 1)
            for t in range(NT):
                pe.wait_ge(xhat_ready, NT * r + t + 1)
                for k in range(KT):
                    if t == 0 and k == 4:
                        pe.wait_ge(gate_ready, 4 * r + 4)
                    ins = pe.transpose(ps[NORM_BANK[k]][:, t * P:(t + 1) * P], xhat[:, t, k * P:(k + 1) * P], ident[:])
                    if t == NT - 1:
                        ins.then_inc(tr_ready, 1)

        def ffn(ph):
            f = ph.index
            s0 = FT * f
            xb = xT_base(3 * (f // 2) + 2 * (f % 2))

            def down(unit, par, count, first, last):
                pe.wait_ge(hid_done, count)
                for t in range(NT):
                    for half in range(2):
                        c = slice(512 * half, 512 * half + 512)
                        tok = slice(t * P, (t + 1) * P)
                        ins = three(ps[2 * t + half][:], split_hi[:, unit.slot, 2, c], split_lo[:, unit.slot, 2, c],
                                    hid_hi[:, par, tok], hid_lo[:, par, tok], first, last, weights_stationary=False)
                ins.then_inc(part_done[2], 1)

            def body(b, first, last):
                for u in range(2):
                    k = u if first else ph.units - 2 + u if last else u
                    body_of = 0 if first or last else b
                    unit = Unit(ph, k, body_of)
                    j = unit.local
                    if not (first and u == 0):
                        pe.wait_ge(silu_done, s0 + j)
                    for q, bank in ((0, BANK_GATE), (1, BANK_UP)):
                        pe.wait_ge(lo_ready, unit.split_count(q))
                        if q == 1 and not (first and u == 0 and f == 0):
                            pe.wait_ge(prod_done, s0 + j)
                        for kk in range(KT):
                            if first and u == 0 and q == 0:
                                pe.wait_ge(xT_ready, xb + kk + 1)
                            w = slice(kk * P, (kk + 1) * P)
                            ins = three(ps[bank][:, 0:T], split_hi[:, unit.slot, q, w], split_lo[:, unit.slot, q, w],
                                        xT_hi[:, kk], xT_lo[:, kk], kk == 0, kk == KT - 1)
                        ins.then_inc(part_done[q], 1)
                    if first and u == 0:
                        continue
                    before = Unit(ph, k - 1, body_of)
                    pe.wait_ge(lo_ready, before.split_count(2))
                    down(before, (u - 1) % 2, s0 + j, first and u == 1, False)
                    if last and u == 1:
                        down(unit, u, s0 + j + 1, False, True)

            bodies(pe, FT // 2, body)

        def proj_a(ph):
            a = ph.index // 3
            xb = xT_base(3 * ph.index + 1)

            def tile(i, w, unit, q):
                pe.wait_ge(lo_ready, unit.split_count(q))
                if not (isinstance(i, int) and i < 3):
                    pe.wait_ge(tile_used, 32 * a + i - 2)
                for k in range(KT):
                    if isinstance(i, int) and i == 0:
                        pe.wait_ge(xT_ready, xb + k + 1)
                    c = slice(k * P, (k + 1) * P)
                    ins = three(ps[PROJ_BANK[w % 3]][:, 0:T], split_hi[:, unit.slot, q, c], split_lo[:, unit.slot, q, c],
                                xT_hi[:, k], xT_lo[:, k], k == 0, k == KT - 1)
                ins.then_inc(part_done[q], 1)

            def body(b, first):
                for u in range(2):
                    unit = Unit(ph, u, 0 if first else b)
                    for q in range(3):
                        w = 3 * u + q
                        tile(w if first else 6 * b + w, w, unit, q)

            body(0, True)
            with pe.Fori(1, 4) as b:
                body(b, False)
            for k in range(8, ph.units):
                unit = Unit(ph, k)
                for q in range(3):
                    i = 3 * k + q
                    if i < 4 * HEADS:
                        tile(i, i, unit, q)
                        for e in (2 * (i - 24), 2 * (i - 24) + 1):
                            pe.wait_ge(sq_ready, 16 * a + e + 1)
                            if e >= 2:
                                pe.wait_ge(r_ready, 16 * a + e - 1)
                            pe.matmul(ps[e % 2][:, 0:T], ones[:], scratch[:, e % 2, 0:T], start=True, stop=True).then_inc(ss_done, 1)
                        continue
                    pe.wait_ge(lo_ready, unit.split_count(q))
                    for t in range(NT):
                        for kk in range(KT):
                            c = slice(kk * AB, (kk + 1) * AB)
                            tok = slice(t * P, (t + 1) * P)
                            ins = three(ps[4][:, t * AB:(t + 1) * AB], split_hi[:, unit.slot, q, c], split_lo[:, unit.slot, q, c],
                                        xT_hi[:, kk, tok], xT_lo[:, kk, tok], kk == 0, kk == KT - 1, weights_stationary=False)
                    ins.then_inc(part_done[2], 1)
            for h in range(2 * HEADS):
                tile_at = (16 + h) if h < HEADS else h
                if h == 0:
                    pe.wait_ge(conv_silu, 24 * a + 24)
                if h >= 2:
                    s, n = (tok_v, h - 1) if h - 2 < HEADS else (tok_k, h - 1 - HEADS)
                    pe.wait_ge(s, HEADS * a + n)
                if h == HEADS:
                    pe.wait_ge(unit_ready, 16 * a + 16)
                    pe.wait_ge(g_ready, a + 1)
                    for c in range(NT):
                        for d in range(2):
                            at = HEADS * (2 * c + d)
                            pe.matmul(ps[4][:, at:at + HEADS], tri[:, d], dn_small[:, SM_G, c, d], start=True, stop=True)
                    pe.matmul(ps[4][:, 48:96], ones[:], dn_small[:, SM_G].rearrange("p c d h -> p (c d h)"),
                              start=True, stop=True).then_inc(gc_done, 1)
                for c in range(NT):
                    ins = pe.transpose(ps[2 + h % 2][:, c * P:(c + 1) * P], qkvz[:, tile_at, c * P:(c + 1) * P], ident[:])
                ins.then_inc(tokT_done, 1)

        def delta_net(layer):
            a = layer // 3
            pe.wait_ge(tok_k, HEADS * a + HEADS)
            pe.wait_ge(tok_v, HEADS * a + HEADS)
            pe.wait_ge(tile_used, 32 * a + 32)
            pe.wait_ge(r_ready, 16 * a + 16)
            pe.wait_ge(state_set, a + 1)
            for pair, (chunks, quad) in enumerate(PAIRS):
                g = 6 * a + pair
                dv = lambda d, n: pe.wait_ge(dn_dve[d], N_DV * g + n)
                po = lambda d, n: pe.wait_ge(dn_pool[d], N_PO * g + n)
                ac = lambda d, n: pe.wait_ge(dn_act[d], N_AC * g + n)

                def four(d, b, lhsT, rhs, transpose=False):
                    for h in range(GROUP):
                        dst = ps[4 * d + b][:, h * P:(h + 1) * P]
                        if transpose:
                            ins = pe.transpose(dst, lhsT(h), ident[:])
                        else:
                            ins = pe.matmul(dst, lhsT(h), rhs(h), start=True, stop=True)
                    ins.then_inc(dn_mm[d], 1)

                def q_of(d, h):
                    return qkvz[:, GROUP * quad + h, chunks[d] * P:(chunks[d] + 1) * P]

                def k_of(d, h):
                    return qkvz[:, HEADS + GROUP * quad + h, chunks[d] * P:(chunks[d] + 1) * P]

                def y_product(d, lev):
                    w = work[d]
                    po(d, po_m(lev))
                    if lev:
                        dv(d, dv_t(lev - 1))
                    if lev:
                        four(d, 0, lambda h: w[W_MASK + lev % 2][:, h], lambda h: w[W_T][:, h])
                    else:
                        four(d, 0, lambda h: w[W_MASK][:, h], None, transpose=True)

                def u_transpose(d, lev):
                    dv(d, dv_t(lev))
                    if lev:
                        ac(d, ac_u(lev - 1))
                    four(d, 2, lambda h: work[d][W_T][:, h], None, transpose=True)

                for d in range(2):
                    dv(d, DV_G4)
                    pe.matmul(ps[4 * d + 2][:], ones[:], work[d][W_Y][:].rearrange("p h c -> p (h c)"),
                              start=True, stop=True).then_inc(dn_mm[d], 1)
                for d in range(2):
                    for h in range(GROUP):
                        pe.matmul(ps[4 * d][:, h * P:(h + 1) * P], k_of(d, h), k_of(d, h), start=True, stop=True)
                    four(d, 1, lambda h: k_of(d, h), lambda h: q_of(d, h))
                for d in range(2):
                    dv(d, DV_A)
                    y_product(d, 0)
                for lev in range(1, LEVELS):
                    for d in range(2):
                        y_product(d, lev)
                        u_transpose(d, lev - 1)
                    for d in range(2):
                        dv(d, dv_y(lev))
                        ac(d, ac_u(lev - 1))
                        dv(d, DV_ATT)
                        four(d, 1, lambda h: work[d][W_U][:, h], lambda h: work[d][W_Y][:, h])
                for d in range(2):
                    u_transpose(d, LEVELS - 1)
                    if pair in (2, 3):
                        pe.wait_ge(state_in, 16 * (4 * a + 2 * quad + 2))
                    four(d, 3, lambda h: k_of(d, h), lambda h: state[:, d, GROUP * quad + h])
                for d in range(2):
                    ac(d, ac_u(LEVELS - 1))
                    four(d, 2, lambda h: q_of(d, h), lambda h: state[:, d, GROUP * quad + h])
                for d in range(2):
                    dv(d, DV_R)
                    four(d, 0, lambda h: work[d][W_U][:, h], lambda h: work[d][W_VB][:, h])
                for d in range(2):
                    ac(d, AC_VN)
                    four(d, 1, lambda h: work[d][W_ATT][:, h], lambda h: work[d][W_VN][:, h])
                for d in range(2):
                    dv(d, DV_VS)
                    four(d, 3, lambda h: dn_k[:, chunks[d], GROUP * quad + h], lambda h: work[d][W_T][:, h])

        def tail(layer, out_ph, o):
            m = tail_index(layer)
            pe.wait_ge(ohat_ready, NT * m + NT)

            def turn(h):
                if h >= 2:
                    pe.wait_ge(on_ready, HEADS * layer + h - 1)
                for t in range(NT):
                    ins = pe.transpose(ps[6 + h % 2][:, t * P:(t + 1) * P], o[:, t, h], ident[:])
                ins.then_inc(otr_ready, 1)

            turn(0)
            turn(1)
            for k in range(HEADS):
                unit, q = Unit(out_ph, k // 3), k % 3
                pe.wait_ge(oT_ready, oT_base(layer) + k + 1)
                pe.wait_ge(lo_ready, unit.split_count(q))
                for t in range(NT):
                    tok = slice(t * P, (t + 1) * P)
                    for half in range(2):
                        c = slice(512 * half, 512 * half + 512)
                        ins = three(ps[2 * t + half][:], split_hi[:, unit.slot, q, c], split_lo[:, unit.slot, q, c],
                                    xT_hi[:, k, tok], xT_lo[:, k, tok], k == 0, k == HEADS - 1, weights_stationary=False)
                ins.then_inc(part_done[q], 1)
                if k + 2 < HEADS:
                    turn(k + 2)

        def attention(ph):
            xb = xT_base(3 * ph.index + 1)
            for k in range(ph.units):
                unit = Unit(ph, k)
                pe.wait_ge(lo_ready, unit.split_count(2))
                for t in range(NT):
                    if NT * k + t >= 3:
                        pe.wait_ge(qkv_copied, NT * k + t - 2)
                    tok = slice(t * P, (t + 1) * P)
                    for kk in range(KT):
                        if k == 0 and t == 0:
                            pe.wait_ge(xT_ready, xb + kk + 1)
                        c = slice(kk * P, (kk + 1) * P)
                        ins = three(ps[PROJ_BANK[t]][:, 0:T].rearrange("p (q c) -> p q c", q=3), split_hi[:, unit.slot, :, c],
                                    split_lo[:, unit.slot, :, c], xT_hi[:, kk, tok], xT_lo[:, kk, tok],
                                    kk == 0, kk == KT - 1, weights_stationary=False)
                    ins.then_inc(part_done[t], 1)
            pe.wait_ge(roped, 4)
            pe.wait_ge(past_in, 32)
            for h in range(HEADS):
                c = slice(h * P, (h + 1) * P)
                if h >= 2:
                    pe.wait_ge(q_head, h - 1)
                    pe.wait_ge(k_head, h - 1)
                for t in range(NT):
                    ins = pe.transpose(ps[h % 2][:, t * P:(t + 1) * P], at_q[:, t, c], ident[:])
                ins.then_inc(head_tr, 1)
                for t in range(NT + 1):
                    src = at_k[:, t, c] if t < NT else past_k[:, c]
                    ins = pe.transpose(ps[2 + h % 2][:, t * P:(t + 1) * P], src, ident[:])
                ins.then_inc(head_tr, 1)
            pe.wait_ge(q_head, HEADS)
            pe.wait_ge(k_head, HEADS)
            items = NT * HEADS
            for i in range(items + 2):
                if i < items:
                    h, t, par = i // NT, i % NT, i % 2
                    if i >= 2:
                        pe.wait_ge(exp_done, i - 1)
                    keys = slice(0, P) if t == 0 else slice(P, T + PAST)
                    n = keys.stop - keys.start
                    for c in range(2):
                        half = slice(DH * c, DH * c + DH)
                        ins = pe.matmul(ps[4 * par + c][:, 0:n], qT[half, h, t * P:(t + 1) * P], kT[half, h, keys], start=True, stop=True)
                    ins.then_inc(score_done, 1)
                if 1 <= i <= items:
                    j = i - 1
                    par, tiles = j % 2, 1 if j % NT == 0 else NT
                    pe.wait_ge(prob_done, j + 1)
                    if j >= 2:
                        pe.wait_ge(pT_copied, j - 1)
                    for b in range(tiles):
                        ins = pe.transpose(ps[4 * par + 2][:, b * P:(b + 1) * P], prob[:, par, 0, b * P:(b + 1) * P], ident[:])
                    ins.then_inc(pT_done, 1)
                if i >= 2:
                    j = i - 2
                    h, t, par = j // NT, j % NT, j % 2
                    pe.wait_ge(pT_copied, j + 1)
                    if j >= 2:
                        pe.wait_ge(ao_copied, j - 1)
                    c = slice(h * P, (h + 1) * P)
                    values = [at_v[:, 0, c]] if t == 0 else [at_v[:, 1, c], at_v[:, 2, c], past_v[:, c]]
                    for b, v in enumerate(values):
                        ins = pe.matmul(ps[4 * par + 3][:, 0:P], probT[:, par, b * P:(b + 1) * P], v, start=b == 0, stop=b == len(values) - 1)
                    ins.then_inc(ao_done, 1)

        def pooling(ph):
            pe.wait_ge(hpad_ready, KT)
            unit = Unit(ph, 0)
            for g in range(4):
                q, side = g // 2, g % 2
                pe.wait_ge(lo_ready, unit.split_count(q))
                pe.wait_ge(oT_ready, oT_base(ph.index) + 2 * g + 2)
                for t in range(NT):
                    tok = slice(t * P, (t + 1) * P)
                    for kk in range(2):
                        c = slice(512 * side + 256 * kk, 512 * side + 256 * kk + 256)
                        ins = three(ps[2 * t + q][:, 256 * side:256 * side + 256], split_hi[:, unit.slot, q, c],
                                    split_lo[:, unit.slot, q, c], xT_hi[:, 2 * g + kk, tok], xT_lo[:, 2 * g + kk, tok],
                                    kk == 0, kk == 1, weights_stationary=False)
                if side:
                    ins.then_inc(part_done[q], 1)


        pe.wait_ge(consts_in, 16 * CONSTS)
        pe.wait_ge(pool_init, 1)
        for r in range(NORMS):
            phs = by_stage[r]
            kind = phs[0].name[0]
            norm(r)
            if kind == "f":
                ffn(phs[0])
            if kind == "a":
                proj_a(phs[0])
                delta_net(r // 3)
                tail(r // 3, phs[1], dn_o)
            if kind == "b":
                attention(phs[0])
                tail(r // 3, phs[1], at_o)
            if kind == "c":
                pooling(phs[0])

    block.__exit__(None, None, None)


def shape_constants():
    i, j = np.meshgrid(np.arange(P), np.arange(P), indexing="ij")
    forward = (i <= j).astype(np.float32)
    tri = np.stack([forward, forward.T], axis=1)
    levels = []
    for lev in range(LEVELS):
        s = 1 << lev
        levels.append((((j // s) % 2 == 1) & (i // s == j // s - 1)).astype(np.float32))
    levels = np.stack(levels, axis=1)
    level_mask = np.stack([levels, levels.transpose(2, 1, 0)], axis=1)
    nf = DH // 4
    inv = (np.float32(10000.0) ** (-np.arange(nf, dtype=np.float32) / np.float32(nf))).astype(np.float32)
    tok = np.arange(TS)
    row = (tok // 64).astype(np.float32)[:, None] * inv
    col = (tok % 64).astype(np.float32)[:, None] * inv
    c = np.concatenate([np.cos(row), np.cos(row), np.cos(col), np.cos(col)], axis=1)
    s = np.concatenate([-np.sin(row), np.sin(row), -np.sin(col), np.sin(col)], axis=1)
    rope = np.stack([c, s], axis=1).astype(np.float32).reshape(2, P, 2, DH).transpose(1, 0, 2, 3)
    counts = np.zeros((4, POOL_OUT), np.float32)
    for g, w in enumerate(POOL_WINDOWS):
        for lo, n in ((0, TP), (TP + POOL_PAD, TS)):
            t = np.arange(n)
            counts[g, lo:lo + n] = 1.0 / (np.clip(t + w // 2, 0, n) - np.clip(t - w // 2, 0, n))
    f = np.ascontiguousarray
    return {"ident": np.eye(P, dtype=np.float32), "tri": f(tri), "level_mask": f(level_mask), "rope_tab": f(rope),
            "inv_count": f(counts.reshape(1, 4 * POOL_OUT))}


def lay_out(a):
    f = np.ascontiguousarray
    a = {k: np.asarray(v) for k, v in a.items()}
    z = shape_constants()
    by_tile = lambda w, n: w.reshape(KT, P, n, P).transpose(2, 1, 0, 3).reshape(n, P, PART)
    ffn = []
    for i in range(DEPTH):
        for h in range(2):
            parts = [by_tile(a["ffn_wg"][i, h], FT), by_tile(a["ffn_wu"][i, h], FT), a["ffn_wd"][i, h].reshape(FT, P, D)]
            ffn.append(np.concatenate(parts, axis=2))
    z["ffn_w"] = np.stack(ffn)
    z["mod_w"] = np.stack([w.T.reshape(MOD_UNITS, MOD_TILES, P, D).transpose(0, 2, 1, 3)
                           .reshape(MOD_UNITS, P, MOD_TILES * D) for w in a["w_mod"]])
    a_in = np.zeros((2, 11, P, 3 * PART), np.float32)
    for s in range(2):
        tiles = by_tile(a["a_w_in"][s][:, :4 * D], 4 * KT)
        a_in[s].reshape(11, P, 3, PART)[:10] = tiles[:30].reshape(10, 3, P, PART).transpose(0, 2, 1, 3)
        a_in[s, 10].reshape(P, 3, PART)[:, :2] = tiles[30:].transpose(1, 0, 2)
        a_in[s, 10, :, 2 * PART:2 * PART + KT * AB] = a["a_w_in"][s][:, 4 * D:].reshape(KT, P, AB).transpose(1, 0, 2).reshape(P, KT * AB)
    z["a_in_w"] = a_in
    rows_of = lambda w: f(w.reshape(KT, P, D).transpose(1, 0, 2).reshape(P, KT * D))
    z["a_out_w"] = np.stack([rows_of(w) for w in a["a_w_out"]])
    z["b_out_w"] = rows_of(a["b_w_out"][0])
    z["b_in_w"] = f(by_tile(a["b_w_qkv"][0], 24).reshape(8, 3, P, PART).transpose(0, 2, 1, 3).reshape(8, P, 3 * PART))
    z["c_w"] = f(a["c_w_pool"][0].reshape(4, 2, P, 256).transpose(2, 0, 1, 3).reshape(P, 2 * PART))
    chan = lambda v: v.reshape(-1, P).T
    z["cond"] = f(np.concatenate([a["c_ctx"], a["c"][0]])[None])
    conv = np.concatenate([a["a_conv"][s].reshape(CONV, 24, P).transpose(2, 1, 0).reshape(P, 24 * CONV) for s in range(2)], axis=1)
    z["cols"] = f(np.concatenate([chan(a["norm_g"]), chan(a["b_mod"]), conv, a["a_norm_g"].T, a["b_norm_g"].T,
                                  chan(a["c_scale"])], axis=1))
    z["rows"] = f(np.concatenate([a["a_A_log"].reshape(-1), a["a_dt_bias"].reshape(-1), a["b_lam"].reshape(-1)])[None])
    z["final_g"] = f(a["final_g"][None])
    z["x_prompt"], z["x_sample"] = f(a["x_prompt"][0]), f(a["x_sample"][0])
    z["state_a"] = f(a["state_a"][0])
    z["past_k"], z["past_v"] = f(a["cache_k"][0, 0].reshape(PAST, D)), f(a["cache_v"][0, 0].reshape(PAST, D))
    return z


OUTS = (("y_prompt", (TP, D)), ("y_sample", (TS, D)), ("state", (2, 2, HEADS, P, P)), ("cache_k", (TP, D)), ("cache_v", (TP, D)))


def program(nc, arrays, stages=3 * DEPTH):
    inp = {n: nc.dram_tensor(n, list(v.shape), F32, kind="ExternalInput").ap() for n, v in arrays.items()}
    out = {n: nc.dram_tensor("out_" + n, list(s), F32, kind="ExternalOutput").ap() for n, s in OUTS}
    build(nc, inp, out, stages)


def kernel(**inputs):
    import concourse.bacc as bacc
    from concourse.bass_utils import run_bass_kernel_spmd

    arrays = lay_out(inputs)
    nc = bacc.Bacc("TRN2", target_bir_lowering=False, num_devices=1)
    program(nc, arrays)
    r = run_bass_kernel_spmd(nc, [arrays], core_ids=[0]).results[0]
    return (r["out_y_prompt"].reshape(1, TP, D), r["out_y_sample"].reshape(1, TS, D),
            r["out_state"].reshape(1, 2, 2, HEADS, P, P), r["out_cache_k"].reshape(1, 1, TP, HEADS, P),
            r["out_cache_v"].reshape(1, 1, TP, HEADS, P))
```

```python
import math

import numpy as np
import concourse.bass as bass
from concourse import mybir
from concourse.alu_op_type import AluOpType as ALU

F32 = mybir.dt.float32
F32R = mybir.dt.float32r
ACT = mybir.ActivationFunctionType
AX = mybir.AxisListType

P = 128
D = 1024
KT = D // P
DEPTH = 4
TP, TS = 128, 256
T = TP + TS
NT = T // P
D_FF = 2816
FT = D_FF // P
N_MOD = 9
EPS = 1e-6
HEADS = D // P
CONV = 5
PAST = 128
DH = 64
CHANNEL_SPANS = ((0, TP), (TP, T))
PART = KT * P
POOL_WINDOWS = (2, 4, 8, 16)
GROUP = 4
LEVELS = 7
AB = 4 * HEADS

MOD_TILES = 2
MOD_UNITS = N_MOD * KT // MOD_TILES
MOD_PROLOGUE = 3 * KT // MOD_TILES
MOD_PER_FFN = 18
MOD_FIRST, MOD_LAST = 2, 4
assert MOD_PROLOGUE + MOD_FIRST + MOD_PER_FFN + MOD_LAST == MOD_UNITS

COL_NORM_G = 0
COL_MOD_B = COL_NORM_G + DEPTH * 3 * KT
COL_CONV = COL_MOD_B + DEPTH * N_MOD * KT
COL_A_NORM = COL_CONV + 2 * 24 * CONV
COL_B_NORM = COL_A_NORM + 2
COL_C_SCALE = COL_B_NORM + 1
COLS = COL_C_SCALE + KT
ROW_A_LOG, ROW_DT, ROW_LAM, ROWS = 0, 32, 64, 64 + 4 * DH

CONV_PAD = CONV // 2
CONV_W = CONV_PAD + TP + CONV_PAD + TS + CONV_PAD
CONV_OUT = CONV_W - 2 * CONV_PAD
CONV_PARTS = ((0, CONV_OUT // 2), (CONV_OUT // 2, CONV_OUT))
CONV_STEPS = (CONV - 1) * len(CONV_PARTS)
POOL_PAD = max(POOL_WINDOWS) // 2
POOL_W = POOL_PAD + TP + POOL_PAD + TS + POOL_PAD
POOL_OUT = POOL_W - 2 * POOL_PAD
SCRATCH_W = 392
LAM_INIT = 0.8 - 0.6 * math.exp(-0.3)
PROBS = 4
AT_NEG_MAX, AT_SUM, AT_RECIP, AT_SCALED, AT_LAM, AT_NEG_LAM, AT_NORM = 16, 24, 32, 40, 44, 46, 47


def weight_phases():
    mixers = (("a_in", 11, 3), ("a_out", 3, 2)), (("b_in", 8, 3), ("b_out", 3, 2)), (("c_in", 1, 2),)
    out = []
    for layer in range(DEPTH):
        out.append(("ffn", FT, 3, 2 * layer))
        out += [(name, units, last, layer) for name, units, last in mixers[layer % 3]]
        out.append(("ffn", FT, 3, 2 * layer + 1))
    return out


class Phase:

    def __init__(self, name, units, last_parts, index, before):
        self.name, self.units, self.last_parts, self.index = name, units, last_parts, index
        self.n0 = before.n0 + before.units if before else 0
        self.parts0 = before.parts0 + 3 * before.units - (3 - before.last_parts) if before else 0
        self.missing0 = 3 * self.n0 - self.parts0


class Unit:

    def __init__(self, phase, k, body=0):
        n = phase.n0 + k
        self.phase, self.k = phase, k
        self.n = n + 2 * body
        self.slot = n % 2
        self.landed = 16 * (n // 2 + body + 1)
        self.local = k + 2 * body
        self.parts_before = phase.parts0 + 3 * (k + 2 * body)
        last = k == phase.units - 1
        self.parts = phase.last_parts if last else 3
        self.first_two = isinstance(self.n, int) and self.n < 2

    def split_count(self, q):
        return self.parts_before + q + 1

    def width(self, q):
        return KT * AB if self.phase.name == "a_in" and self.k == self.phase.units - 1 and q == 2 else PART


def build(nc, inp, out, stages=3 * DEPTH):
    phases = []
    for name, units, last, index in weight_phases():
        phases.append(Phase(name, units, last, index, phases[-1] if phases else None))

    def stage_of(ph):
        return 3 * (ph.index // 2) + 2 * (ph.index % 2) if ph.name == "ffn" else 3 * ph.index + 1

    phases = [ph for ph in phases if stage_of(ph) < stages]
    by_stage = {}
    for ph in phases:
        by_stage.setdefault(stage_of(ph), []).append(ph)

    def phase_of(n):
        return next(ph for ph in phases if ph.n0 <= n < ph.n0 + ph.units)

    def following(unit):
        n = unit.n + 1
        if n >= phases[-1].n0 + phases[-1].units:
            return None
        nxt = phase_of(n)
        return Unit(nxt, n - nxt.n0)

    def release(unit, q):
        if isinstance(unit.n, int):
            ph = phase_of(unit.n - 2)
        else:
            ph = unit.phase
        which = 2 if ph.name == "b_in" else q
        n = unit.n - 2
        if isinstance(unit.n, int):
            old = Unit(ph, n - ph.n0)
            if q >= old.parts:
                which = 1
        return which, n + 1 - (ph.missing0 if which == 2 else 0)

    def done(unit, q):
        return unit.n + 1 - (unit.phase.missing0 if q == 2 else 0)

    def mod_steps(f, b, first, last):
        if f >= 7:
            return []
        layer = (f + 1) // 2
        if f:
            m0 = MOD_UNITS + MOD_PER_FFN * (f - 1)
        else:
            m0 = MOD_PROLOGUE + MOD_FIRST
        if not first and not last:
            return [(u, m0 + u + 2 * (b - 1), (m0 + u) % 2, 16 * ((m0 + u - MOD_PROLOGUE) // 2 + 1 + b), layer) for u in range(2)]
        if f:
            return []
        start, count = (MOD_PROLOGUE, MOD_FIRST) if first else (MOD_UNITS - MOD_LAST, MOD_LAST)
        return [(0 if first else i // 2, start + i, (start + i) % 2, 16 * ((start + i - MOD_PROLOGUE) // 2 + 2), layer) for i in range(count)]

    NORMS = stages

    def sub_base(r):
        return (NT - 1) * (r - (r > 7))

    def oT_base(layer):
        return KT * layer

    def xT_base(r):
        return KT * (r - (r > 7))

    base = nc.sbuf_base + (-nc.sbuf_base) % 64
    top = [base]

    def place(name, shape, dtype=F32, at=None):
        size = int(np.prod(shape[1:])) * 4
        if at is None:
            at = top[0]
            top[0] += size + (-size) % 32
        assert at + size <= nc.sbuf_usable_end, (name, at + size, nc.sbuf_usable_end)
        return nc.alloc_sbuf_tensor_at(name, shape, dtype, offset=at)

    raw = place("raw", [P, 2, 3, PART])
    region_m = top[0]
    mod_raw = place("mod_raw", [P, 2, MOD_TILES, D])
    x = place("x", [P, NT, D])
    region_a = top[0]
    xT_hi = place("xT_hi", [P, KT, T], F32R)
    xT_lo = place("xT_lo", [P, KT, T], F32R)
    gate_bc = place("gate_bc", [P, 2, D])
    ident = place("ident", [P, P])
    ones = place("ones", [P, P])
    tri = place("tri", [P, 2, P])
    cond = place("cond", [P, 2, D])
    rope_tab = place("rope_tab", [P, 2, 2, DH])
    cols = place("cols", [P, COLS])
    rows = place("rows", [P, ROWS])
    modv = place("modv", [P, 2, N_MOD * KT, 2])
    scale_col = place("scale_col", [P, KT, 2])
    gate_col = place("gate_col", [P, KT, 2])
    sumsq = place("sumsq", [P, NT * HEADS])
    rstd = place("rstd", [P, NT * HEADS])
    neg_half = place("neg_half", [P, NT * HEADS])
    bias_eps = place("bias_eps", [P, 1])
    dn_small = place("dn_small", [P, 12, NT, 2, HEADS])
    ab_rows = place("ab_rows", [P, T])
    at_small = place("at_small", [P, 64])
    lam_prod = place("lam_prod", [P, 2, DH])
    region_w = top[0]
    split_hi = place("split_hi", [P, 2, 3, PART], F32R)
    split_lo = place("split_lo", [P, 2, 3, PART], F32R)
    region_r = top[0]
    KB = 1024
    scratch = place("scratch", [P, 4, SCRATCH_W], at=region_r + 48 * KB)
    diag = place("diag", [P, 2, KT, P], at=region_r)
    res_tmp = place("res_tmp", [P, 3, 512], at=region_r + 12 * KB)
    xhat = place("xhat", [P, NT, D], at=region_r + 24 * KB)
    silu_g = place("silu_g", [P, 2, T], at=region_r + 36 * KB)
    hidden = place("hidden", [P, 2, T], at=region_r + 39 * KB)
    hid_hi = place("hid_hi", [P, 2, T], F32R, at=region_r + 42 * KB)
    hid_lo = place("hid_lo", [P, 2, T], F32R, at=region_r + 45 * KB)
    final_row = place("final_row", [P, D], at=region_r)
    mod_junk = place("mod_junk", [P, D], at=region_r + 8 * KB)
    mod_prod = place("mod_prod", [P, 2, D], at=region_r + 24 * KB)
    mod_at = [region_w + 8 * KB * i for i in range(6)] + [region_a + 8 * KB * i for i in range(4)]
    mod_first = [place(f"mod_first{i}", [P, MOD_TILES, D], at=at) for i, at in enumerate(mod_at)]
    level_mask = place("level_mask", [P, 2, LEVELS, P], at=region_m + 8 * KB)
    qkvz = place("qkvz", [P, 4 * HEADS, T], at=region_r)
    dn_o = place("dn_o", [P, NT, HEADS, P], at=region_r + 24 * KB)
    dn_k = place("dn_k", [P, NT, HEADS, P], at=region_a)
    dn_v = place("dn_v", [P, NT, HEADS, P], at=region_a + 12 * KB)
    state = place("state", [P, 2, HEADS, P], at=region_w)
    work = [[place(f"work_{d}_{i}", [P, GROUP, P], at=region_w + (8 + 20 * d + 2 * i) * KB) for i in range(10)]
            for d in range(2)]
    sq_tmp = place("sq_tmp", [P, NT, HEADS, P], at=region_r + 12 * KB)
    at_q = place("at_q", [P, NT, D], at=region_r)
    at_k = place("at_k", [P, NT, D], at=region_r + 12 * KB)
    at_v = place("at_v", [P, NT, D], at=region_r + 24 * KB)
    past_k = place("past_k", [P, D], at=region_r + 36 * KB)
    past_v = place("past_v", [P, D], at=region_r + 40 * KB)
    at_o = place("at_o", [P, NT, HEADS, P], at=region_r)
    rope_a = place("rope_a", [P, D], at=region_r + 44 * KB)
    rope_b = place("rope_b", [P, D], at=region_r + 48 * KB)
    qT = place("qT", [P, HEADS, T], at=region_w)
    kT = place("kT", [P, HEADS, T + PAST], at=region_w + 12 * KB)
    prob = place("prob", [P, PROBS, 2, T], at=region_w + 28 * KB)
    probT = place("probT", [P, 2, T], at=region_w + 40 * KB)
    hpad = place("hpad", [P, KT, POOL_W], at=region_r)
    pool_tmp = place("pool_tmp", [P, 3, POOL_W], at=region_r + 14 * KB)
    inv_count = place("inv_count", [P, 4, POOL_OUT], at=region_r + 36 * KB)

    ps = [nc.alloc_psum_tensor(f"bank{i}", [P, 512], F32) for i in range(8)]
    BANK_GATE, BANK_UP = 6, 7
    NORM_BANK = (6, 7, 4, 5, 0, 1, 2, 3)
    PROJ_BANK = (6, 7, 5)

    sem = nc.alloc_semaphore
    consts_in = sem("consts_in")
    x_in = sem("x_in")
    cond_in, cond_ready = sem("cond_in"), sem("cond_ready")
    pool_init = sem("pool_init")
    raw_landed = [sem(f"raw_landed{i}") for i in range(2)]
    hi_ready, lo_ready = sem("hi_ready"), sem("lo_ready")
    part_done = [sem(f"part_done{q}") for q in range(3)]
    mod_landed = [sem(f"mod_landed{i}") for i in range(2)]
    mod_first_landed = [sem(f"mod_first_landed{i}") for i in range(len(mod_first))]
    mod_first_sum = {e: sem(f"mod_first_{e}") for e in ("dve", "mult", "act")}
    mod_sum = {e: sem(f"mod_{e}") for e in ("dve", "mult", "act")}
    mask_in = sem("mask_in")
    scale_ready, diag_ready = sem("scale_ready"), sem("diag_ready")
    gate_mm, gate_ready = sem("gate_mm"), sem("gate_ready")
    res_prod, res_pool, res_dve = sem("res_prod"), sem("res_pool"), sem("res_dve")
    sumsq_ready, rstd_ready, xhat_ready = sem("sumsq_ready"), sem("rstd_ready"), sem("xhat_ready")
    sub_done, first_tap = sem("sub_done"), sem("first_tap")
    tr_ready, xn_ready, xT_ready = sem("tr_ready"), sem("xn_ready"), sem("xT_ready")
    silu_done, prod_done, hid_hi_done, hid_done = (sem(s) for s in ("silu_done", "prod_done", "hid_hi_done", "hid_done"))
    dve_seq, act_seq, pool_seq = sem("dve_seq"), sem("act_seq"), sem("pool_seq")
    y_ready, stored = sem("y_ready"), sem("stored")
    oss_ready, orstd_ready, ohat_ready = sem("oss_ready"), sem("orstd_ready"), sem("ohat_ready")
    otr_ready, on_ready, ohi_ready, oT_ready = sem("otr_ready"), sem("on_ready"), sem("ohi_ready"), sem("oT_ready")
    osq_ready = sem("osq_ready")
    pad_zero, tile_used, conv_step, conv_silu = (sem(n) for n in ("pad_zero", "tile_used", "conv_step", "conv_silu"))
    sq_ready, ss_done, r_ready, unit_ready, z_ready = (sem(n) for n in ("sq_ready", "ss_done", "r_ready", "unit_ready", "z_ready"))
    tokT_done, tok_v, tok_k = sem("tokT_done"), sem("tok_v"), sem("tok_k")
    ab_rows_ready, ab_turned = sem("ab_rows_ready"), sem("ab_turned")
    ab_in, ab_exp, g_ready, gc_done = sem("ab_in"), sem("ab_exp"), sem("g_ready"), sem("gc_done")
    decay_in, decay_out, small_ready = sem("decay_in"), sem("decay_out"), sem("small_ready")
    state_in, state_set, state_stored = sem("state_in"), sem("state_set"), sem("state_stored")
    dn_mm, dn_dve, dn_act, dn_pool, dn_sum = ([sem(f"dn_{e}{d}") for d in range(2)] for e in ("mm", "dve", "act", "pool", "sum"))
    pre_mm, pre_dve, pre_act, pre_pool = ([sem(f"pre_{e}{d}") for d in range(2)] for e in ("mm", "dve", "act", "pool"))
    qkv_copied, past_in, roped, lam_ready, lam_exp = (sem(s) for s in ("qkv_copied", "past_in", "roped", "lam_ready", "lam_exp"))
    cache_out = sem("cache_out")
    head_tr, q_head, k_head = sem("head_tr"), sem("q_head"), sem("k_head")
    score_done, max_done, exp_done, prob_done = (sem(s) for s in ("score_done", "max_done", "exp_done", "prob_done"))
    pT_done, pT_copied, ao_done, ao_copied = (sem(s) for s in ("pT_done", "pT_copied", "ao_done", "ao_copied"))
    hpad_zero, hpad_ready, count_in = sem("hpad_zero"), sem("hpad_ready"), sem("count_in")

    CONSTS = 5

    def f32(ap):
        return ap.bitcast(F32)

    def vec_of(r):
        return r // 3 % 2, 3 * KT * (r % 3)

    def mod_needed(r):
        layer, which = divmod(r, 3)
        return MOD_UNITS * layer + (which + 1) * 3 * KT // MOD_TILES

    def mod_operand(m):
        if m < len(mod_first):
            return mod_first[m][:], mod_first_landed[m], 16
        return mod_raw[:, m % 2], mod_landed[m % 2], 16 * ((m - len(mod_first)) // 2 + 1)

    def in_prologue(m):
        return isinstance(m, int) and m < MOD_PROLOGUE

    def mod_count(which, m, i=0):
        if isinstance(m, int) and m <= MOD_PROLOGUE and not (m == MOD_PROLOGUE and i):
            return mod_first_sum[which], (3 if which == "dve" else 1) * m + i
        return mod_sum[which], 2 * (m - MOD_PROLOGUE) + i

    def mod_column(layer, unit, t, c):
        return modv[:, layer % 2, bass.ds(MOD_TILES * unit + t, 1), c:c + 1].rearrange("p t c -> p (t c)")

    def mod_dve(eng, weights, landed, count, m, layer, unit):
        eng.wait_ge(landed, count)
        for i, (t, c) in enumerate(((0, 0), (1, 0), (0, 1)) if in_prologue(m) else ((0, 0), (1, 0))):
            if not (isinstance(m, int) and m == 0 and i == 0):
                eng.wait_ge(*mod_count("dve", m, i))
            eng.scalar_tensor_tensor(mod_junk[:], weights[:, t], 1.0, cond[:, c], ALU.mult, ALU.mult,
                                     accum_out=mod_column(layer, unit, t, c)).then_inc(mod_count("dve", m, 1)[0], 1)

    def mod_pool(eng, weights, landed, count, m):
        eng.wait_ge(landed, count)
        for i, t in enumerate((1,) if in_prologue(m) else (0, 1)):
            if not in_prologue(m):
                if isinstance(m, int) and m == MOD_PROLOGUE:
                    eng.wait_ge(*mod_count("act", m))
                else:
                    eng.wait_ge(*mod_count("act", m - 1, i + 1))
            elif m >= 2:
                eng.wait_ge(*mod_count("act", m - 1))
            buf = mod_prod[:, m % 2 if in_prologue(m) else i]
            eng.tensor_tensor(buf, weights[:, t], cond[:, 1], ALU.mult).then_inc(mod_count("mult", m, 1)[0], 1)

    def mod_act(eng, m, layer, unit):
        for i, t in enumerate((1,) if in_prologue(m) else (0, 1)):
            eng.wait_ge(*mod_count("mult", m, i + 1))
            buf = mod_prod[:, m % 2 if in_prologue(m) else i]
            eng.activation(buf, buf, ACT.Copy, accum_out=mod_column(layer, unit, t, 1)).then_inc(mod_count("act", m, 1)[0], 1)

    def mod_before(r):
        ffns = 2 * (r // 3) + (r % 3 + 1) // 2
        return MOD_UNITS + MOD_PER_FFN * (min(ffns, 7) - 1) if ffns else MOD_PROLOGUE

    def bodies(eng, count, body):
        body(0, True, False)
        with eng.Fori(1, count - 1) as b:
            body(b, False, False)
        body(count - 1, False, True)

    class Steps:

        def __init__(self, eng, s):
            self.eng, self.s, self.n = eng, s, 0

        def settle(self, ins):
            self.n += 1
            ins.then_inc(self.s, 1)
            self.eng.wait_ge(self.s, self.n)

    PAIRS = [((0, 0), 0), ((0, 0), 1), ((1, 2), 0), ((1, 2), 1), ((2, 1), 0), ((2, 1), 1)]
    (W_Y, W_E, W_A, W_ATT, W_T, W_U, W_VB, W_VN, W_MASK) = range(9)
    PM_D, PM_KK, PM_KQ, N_PM = 1, 2, 3, 3
    PV_G4, PV_ARG, PV_MIN, PV_A, PV_ATT, N_PV = 1, 2, 3, 4, 5, 5
    MM_Y0, MM_U6, MM_KS, MM_QS, MM_VN, MM_OI, MM_DS = 1, 20, 21, 22, 23, 24, 25
    mm_y = lambda lev: 3 * lev - 1 if lev else MM_Y0
    mm_z = lambda lev: 3 * lev + 1
    mm_u = lambda lev: 3 * lev + 3 if lev < LEVELS - 1 else MM_U6
    DV_KS, DV_R, DV_QS, DV_VS, DV_O, DV_STATE = 15, 16, 17, 18, 19, 20
    dv_y = lambda lev: 2 * lev + 1
    dv_t = lambda lev: 2 * lev + 2
    AC_VN = 8
    ac_u = lambda lev: lev + 1
    PO_VB, PO_STATE = 3, 9
    po_m = lambda lev: lev + 1 if lev < 2 else lev + 2
    N_MM, N_DV, N_AC, N_PO = 25, 20, 8, 9
    SM_X, SM_G, SM_GC, SM_TOTAL, SM_EG, SM_GLAST, SM_EKD, SM_BEG, SM_BETA, SM_B, SM_ABS = range(11)

    def small(which, c, d, quad):
        v = dn_small[:, which, c, d, GROUP * quad:GROUP * quad + GROUP]
        return v.rearrange("p (h o) -> p h o", o=1).to_broadcast([P, GROUP, P])

    def per_head(ap):
        return ap.rearrange("p (o c) -> p o c", o=1).to_broadcast([P, GROUP, P])

    def writes_first(pair, d):
        return d == 0 if pair < 2 else pair < 4

    def from_nothing(pair):
        return pair < 2

    def heads_of(quad):
        return slice(GROUP * quad, GROUP * quad + GROUP)

    def tail_index(layer):
        return layer - (layer > 2)

    block = nc.Block()
    block.__enter__()

    @block.sync
    def _(sp):
        def load_unit(unit):
            if not unit.first_two:
                if isinstance(unit.n, int):
                    ph = phase_of(unit.n - 2)
                    old = Unit(ph, unit.n - 2 - ph.n0)
                    sp.wait_ge(lo_ready, old.split_count(old.parts - 1))
                else:
                    sp.wait_ge(lo_ready, unit.parts_before - 3)
            ph = unit.phase
            width = sum(unit.width(q) for q in range(unit.parts))
            dst = raw[:, unit.slot].rearrange("p q c -> p (q c)")[:, 0:width]
            if ph.name == "ffn":
                src = inp["ffn_w"][ph.index, bass.ds(unit.local, 1)].rearrange("u p c -> (u p) c")
            elif ph.name == "a_in":
                src = inp["a_in_w"][ph.index // 3, bass.ds(unit.local, 1)].rearrange("u p c -> (u p) c")[:, 0:width]
            elif ph.name == "b_in":
                src = inp["b_in_w"][bass.ds(unit.local, 1)].rearrange("u p c -> (u p) c")
            elif ph.name == "a_out":
                src = inp["a_out_w"][ph.index // 3, :, unit.k * 3 * PART:unit.k * 3 * PART + width]
            elif ph.name == "b_out":
                src = inp["b_out_w"][:, unit.k * 3 * PART:unit.k * 3 * PART + width]
            else:
                src = inp["c_w"]
            sp.dma_start(dst, src).then_inc(raw_landed[unit.slot], 16)

        def load_mod(m, slot, layer, unit):
            sp.wait_ge(*mod_count("dve", m - 1))
            sp.wait_ge(*mod_count("mult", m - 1))
            src = inp["mod_w"][layer, bass.ds(unit, 1)].rearrange("u p c -> (u p) c")
            sp.dma_start(mod_raw[:, slot].rearrange("p t c -> p (t c)"), src).then_inc(mod_landed[slot], 16)

        sp.dma_start(cond[:].rearrange("p c k -> p (c k)"), inp["cond"].to_broadcast([P, 2 * D])).then_inc(cond_in, 16)
        for m in range(MOD_PROLOGUE):
            dst, landed, _ = mod_operand(m)
            sp.dma_start(dst.rearrange("p t c -> p (t c)"), inp["mod_w"][0, m]).then_inc(landed, 16)
            if m >= MOD_PROLOGUE - 2:
                load_unit(Unit(phases[0], m - MOD_PROLOGUE + 2))
        for stage in range(NORMS):
            for ph in by_stage[stage]:
                if ph.name == "ffn":
                    f = ph.index

                    def load_body(b, first, last):
                        if f == 1 and first:
                            for d in range(2):
                                sp.wait_ge(dn_pool[d], 6 * N_PO)
                        if last:
                            load_unit(Unit(ph, ph.units - 2))
                            load_unit(Unit(ph, ph.units - 1))
                        for u in range(2):
                            if not (ph.n0 == 0 and first) and not last:
                                load_unit(Unit(ph, u, 0 if first else b))
                            for step, m, slot, _, layer in mod_steps(f, b, first, last):
                                if step == u:
                                    load_mod(m, slot, layer, m - MOD_UNITS * layer)
                            if f == 0 and last and u == 0 and stages > 1:
                                load_unit(Unit(by_stage[1][0], 0))

                    bodies(sp, FT // 2, load_body)
                elif ph.name == "a_out":
                    a = ph.index // 3
                    load_unit(Unit(ph, 0))
                    load_unit(Unit(ph, 1))
                    for quad in range(2):
                        hs = heads_of(quad)
                        for d in range(2):
                            sp.wait_ge(dn_dve[d], N_DV * (6 * a + quad) + DV_STATE)
                            sp.dma_start(out["state"][a, d, hs].rearrange("h k v -> k h v"), state[:, d, hs]).then_inc(state_stored, 16)
                        sp.wait_ge(state_stored, 16 * (4 * a + 2 * quad + 2))
                        for d in range(2):
                            sp.dma_start(state[:, d, hs], inp["state_a"][a, d, hs].rearrange("h k v -> k h v")).then_inc(state_in, 16)
                    load_unit(Unit(ph, 2))
                elif ph.name == "a_in":
                    def load_pair(b, first, last):
                        for u in range(2):
                            load_unit(Unit(ph, u, 0 if first else b))
                    if ph.index:
                        load_unit(Unit(ph, 0))
                    load_unit(Unit(ph, 1))
                    with sp.Fori(1, 4) as b:
                        load_pair(b, False, False)
                    for k in range(8, ph.units):
                        load_unit(Unit(ph, k))
                else:
                    for k in range(ph.units):
                        load_unit(Unit(ph, k))
        sp.wait_ge(stored, 16 * NT)

    @block.gpsimd
    def _(pool):
        steps = Steps(pool, pool_seq)
        pool.dma_start(cols[:], inp["cols"]).then_inc(consts_in, 16)
        pool.dma_start(ident[:], inp["ident"]).then_inc(consts_in, 16)
        for t in range(NT):
            src = inp["x_prompt"] if t == 0 else inp["x_sample"][(t - 1) * P:t * P]
            pool.dma_start(x[:, t], src).then_inc(x_in, 16)
        pool.dma_start(tri[:], inp["tri"]).then_inc(consts_in, 16)
        pool.dma_start(rope_tab[:], inp["rope_tab"]).then_inc(consts_in, 16)
        pool.dma_start(rows[:], inp["rows"].to_broadcast([P, ROWS])).then_inc(consts_in, 16)
        pool.memset(ones[:], 1.0)
        pool.memset(bias_eps[:], EPS)
        pool.memset(neg_half[:], -0.5).then_inc(pool_init, 1)
        pool.wait_ge(pool_init, 1)

        def root(span, mean_of, ready):
            steps.settle(pool.tensor_scalar(rstd[:, span], sumsq[:, span], 1.0 / mean_of, EPS, ALU.mult, ALU.add))
            pool.tensor_tensor(rstd[:, span], rstd[:, span], neg_half[:, span], ALU.pow).then_inc(ready, 1)

        def norm_root(r):
            for t in range(NT):
                pool.wait_ge(sumsq_ready, NT * r + t + 1)
                root(slice(t, t + 1), D, rstd_ready)

        def residual(r):
            for t in range(NT):
                pool.wait_ge(res_prod, 6 * r + 2 * t + 1)
                pool.tensor_tensor(x[:, t, 0:512], x[:, t, 0:512], res_tmp[:, 2 * t % 3], ALU.add).then_inc(res_pool, 1)

        def mixer_root(layer):
            i = tail_index(layer)
            for t in range(NT):
                pool.wait_ge(oss_ready, NT * i + t + 1)
                root(slice(HEADS * t, HEADS * t + HEADS), P, orstd_ready)

        def pool_setup(r):
            pool.dma_start(inv_count[:].rearrange("p g t -> p (g t)"),
                           inp["inv_count"].to_broadcast([P, 4 * POOL_OUT])).then_inc(count_in, 16)
            pool.wait_ge(gate_mm, 4 * r + 4)
            pool.wait_ge(res_dve, NT * r)
            pool.memset(hpad[:], 0.0).then_inc(hpad_zero, 1)

        def attention(layer):
            pool.dma_start(past_k[:], inp["past_k"]).then_inc(past_in, 16)
            pool.dma_start(past_v[:], inp["past_v"]).then_inc(past_in, 16)
            pool.wait_ge(qkv_copied, 8 * NT)
            pool.dma_start(out["cache_k"], at_k[:, 0]).then_inc(cache_out, 16)
            pool.dma_start(out["cache_v"], at_v[:, 0]).then_inc(cache_out, 16)

        def ffn(f):
            pool.wait_ge(tr_ready, KT * (3 * (f // 2) + 2 * (f % 2)) + KT)

            def body(b, first, last):
                for _, m, slot, landed, layer in mod_steps(f, b, first, last):
                    mod_pool(pool, mod_raw[:, slot], mod_landed[slot], landed, m)
            bodies(pool, FT // 2, body)

        def delta_net(layer):
            a = layer // 3
            pool.wait_ge(*mod_count("dve", MOD_UNITS * (DEPTH if a else 1)))
            pool.dma_start(level_mask[:], inp["level_mask"]).then_inc(mask_in, 16)
            pool.wait_ge(mask_in, 16 * (a + 1))
            pool.wait_ge(xT_ready, xT_base(3 * layer + 1) + KT)
            pool.memset(scratch[:, 0:2], 0.0).then_inc(pad_zero, 1)
            pool.wait_ge(gc_done, a + 1)
            pool.memset(state[:], 0.0).then_inc(state_set, 1)
            pool.wait_ge(tok_v, KT * a + KT)
            pool.wait_ge(small_ready, a + 1)

            def prepare(pair):
                for d in range(2):
                    e = work[d][W_Y][:]
                    pool.wait_ge(pre_act[d], 6 * a + pair + 1)
                    pool.tensor_tensor(e, e, per_head(tri[:, d]), ALU.mult).then_inc(pre_pool[d], 1)

            def add_directions(pair):
                chunks, quad = PAIRS[pair]
                g = 6 * a + pair
                for d in range(2):
                    if not writes_first(pair, d):
                        pool.wait_ge(dn_dve[1 - d], N_DV * (g if pair < 2 else g - 2) + DV_O)
                        pool.wait_ge(dn_dve[d], N_DV * g + DV_O)
                        o = dn_o[:, chunks[d], heads_of(quad)]
                        pool.tensor_tensor(o, o, work[d][W_E][:], ALU.add).then_inc(dn_sum[d], 1)

            prepare(0)
            for pair, (chunks, quad) in enumerate(PAIRS):
                g = 6 * a + pair
                hs = heads_of(quad)
                for lev in range(LEVELS):
                    if lev == 3 and pair:
                        add_directions(pair - 1)
                    for d in range(2):
                        w = work[d]
                        if lev == 2:
                            beta = small(SM_BETA, chunks[d], d, quad)
                            pool.tensor_tensor(w[W_VB][:], dn_v[:, chunks[d], hs], beta, ALU.mult).then_inc(dn_pool[d], 1)
                        if lev == 0:
                            pool.wait_ge(pre_dve[d], N_PV * g + PV_A)
                        if lev >= 2:
                            pool.wait_ge(dn_mm[d], N_MM * g + mm_y(lev - 2))
                        pool.tensor_tensor(w[W_MASK + lev % 2][:], w[W_A][:], per_head(level_mask[:, d, lev]),
                                           ALU.mult).then_inc(dn_pool[d], 2 if from_nothing(pair) and lev == LEVELS - 1 else 1)
                for d in range(0 if from_nothing(pair) else 2):
                    pool.wait_ge(dn_mm[d], N_MM * g + MM_QS)
                    pool.tensor_tensor(state[:, d, hs], state[:, d, hs], small(SM_GLAST, chunks[d], d, quad),
                                       ALU.mult).then_inc(dn_pool[d], 1)
                if pair + 1 < len(PAIRS):
                    prepare(pair + 1)
            add_directions(len(PAIRS) - 1)

        for m in range(MOD_PROLOGUE):
            if m == 0:
                pool.wait_ge(cond_ready, 1)
            mod_pool(pool, *mod_operand(m), m)
        for r in range(NORMS):
            kind = ("ffn", "abca"[r // 3], "ffn")[r % 3]
            norm_root(r)
            if kind == "ffn" and r < 3 * DEPTH - 1:
                ffn(2 * (r // 3) + r % 3 // 2)
            if kind == "c":
                pool_setup(r)
            if kind == "a":
                delta_net(r // 3)
                mixer_root(r // 3)
            if kind == "b":
                attention(r // 3)
                mixer_root(r // 3)
            residual(r)
        pool.wait_ge(gate_mm, 4 * NORMS)
        pool.dma_start(final_row[:], inp["final_g"].to_broadcast([P, D])).then_inc(count_in, 16)
        norm_root(NORMS)
        for t in range(NT):
            pool.wait_ge(y_ready, t + 1)
            dst = out["y_prompt"] if t == 0 else out["y_sample"][(t - 1) * P:t * P]
            pool.dma_start(dst, xhat[:, t]).then_inc(stored, 16)

    @block.scalar
    def _(act):
        steps = Steps(act, act_seq)

        def round_part(unit, q):
            if q >= unit.parts:
                return
            if q == 0:
                act.wait_ge(raw_landed[unit.slot], unit.landed)
            if not unit.first_two:
                which, count = release(unit, q)
                act.wait_ge(part_done[which], count)
            w = unit.width(q)
            act.activation(split_hi[:, unit.slot, q, 0:w], raw[:, unit.slot, q, 0:w], ACT.Copy).then_inc(hi_ready, 1)

        def round_unit(unit):
            for q in range(3):
                round_part(unit, q)

        act.wait_ge(cond_in, 16)
        act.activation(cond[:], cond[:], ACT.Silu).then_inc(cond_ready, 1)
        for m in range(MOD_PROLOGUE):
            mod_act(act, m, 0, m)
            if m == MOD_PROLOGUE // 2:
                act.wait_ge(x_in, 16 * NT)
                for t in range(NT):
                    if t:
                        act.wait_ge(sumsq_ready, t)
                    act.activation(scratch[:].rearrange("p r c -> p (r c)")[:, 0:D], x[:, t], ACT.Square,
                                   accum_out=sumsq[:, t:t + 1]).then_inc(sumsq_ready, 1)
        act.wait_ge(*mod_count("dve", len(mod_first)))
        act.wait_ge(consts_in, 16 * CONSTS)
        round_unit(Unit(phases[0], 0))

        def gate_rows(r):
            for i in range(4):
                act.wait_ge(gate_mm, 4 * r + i + 1)
                act.activation(gate_bc[:, i // 2, (i % 2) * 512:(i % 2) * 512 + 512], ps[i][:], ACT.Copy).then_inc(gate_ready, 1)

        def norm(r, to_pad=False):
            act.wait_ge(*mod_count("act", mod_before(r)))
            for t in range(NT if r else 0):
                act.wait_ge(res_pool, NT * (r - 1) + t + 1)
                act.wait_ge(res_dve, NT * (r - 1) + t + 1)
                act.activation(xhat[:, t], x[:, t], ACT.Square, accum_out=sumsq[:, t:t + 1]).then_inc(sumsq_ready, 1)
            if r == NORMS:
                return
            if r:
                gate_rows(r)
            par, v0 = vec_of(r)
            act.wait_ge(scale_ready, r + 1)
            for k in range(KT):
                if r == 0 and k == KT // 2:
                    gate_rows(0)
                act.wait_ge(tr_ready, KT * r + k + 1)
                if k >= 4 and not to_pad:
                    act.wait_ge(xT_ready, xT_base(r) + k - 3)
                if k == 0 and to_pad:
                    act.wait_ge(hpad_zero, 1)
                for c, (lo, hi) in enumerate(CHANNEL_SPANS):
                    pad = POOL_PAD * (c + 1)
                    dst = hpad[:, k, lo + pad:hi + pad] if to_pad else scratch[:, k % 4, lo:hi]
                    ins = act.activation(dst, ps[NORM_BANK[k]][:, lo:hi], ACT.Identity,
                                         bias=modv[:, par, v0 + k, c:c + 1], scale=scale_col[:, k, c:c + 1])
                ins.then_inc(hpad_ready if to_pad else xn_ready, 1)

        def ffn(ph):
            f = ph.index
            s0 = FT * f

            def body(b, first, last):
                for u in range(2):
                    k = u if first else ph.units - 2 + u if last else u
                    unit = Unit(ph, k, 0 if first or last else b)
                    nxt = following(unit) if (last and u == 1) else Unit(ph, k + 1, 0 if first or last else b)
                    j = unit.local
                    par = u % 2
                    if nxt:
                        round_part(nxt, 0)
                        round_part(nxt, 1)
                    act.wait_ge(part_done[0], done(unit, 0))
                    if not (first and f == 0):
                        act.wait_ge(prod_done, s0 + j - 1)
                    act.activation(silu_g[:, par], ps[BANK_GATE][:, 0:T], ACT.Silu).then_inc(silu_done, 1)
                    act.wait_ge(prod_done, s0 + j + 1)
                    if not (first):
                        act.wait_ge(part_done[2], done(unit, 2) - 2)
                    act.activation(hid_hi[:, par], hidden[:, par], ACT.Copy).then_inc(hid_hi_done, 1)
                    if nxt:
                        round_part(nxt, 2)
                    for step, m, _, _, layer in mod_steps(f, b, first, last):
                        if step == u:
                            mod_act(act, m, layer, m - MOD_UNITS * layer)

            bodies(act, FT // 2, body)

        def proj_a(ph):
            a = ph.index // 3

            def copy_padded(i, w, unit, q):
                act.wait_ge(part_done[q], done(unit, q))
                if not (isinstance(i, int) and i < 2):
                    act.wait_ge(conv_step, CONV_STEPS * (24 * a + i - 1))
                for c, (lo, hi) in enumerate(CHANNEL_SPANS):
                    pad = CONV_PAD * (c + 1)
                    ins = act.activation(scratch[:, w % 2, lo + pad:hi + pad], ps[PROJ_BANK[w % 3]][:, lo:hi], ACT.Copy)
                ins.then_inc(tile_used, 1)
                if not (isinstance(i, int) and i < 2):
                    act.wait_ge(conv_silu, 24 * a + i - 1)
                elif a:
                    act.wait_ge(conv_silu, 24 * a)
                act.wait_ge(tile_used, 32 * a + i + 1)
                weight = cols[:, bass.ds(COL_CONV + 24 * CONV * a + CONV * i, 1)]
                act.activation(scratch[:, 2 + w % 2, 0:CONV_OUT], scratch[:, w % 2, 0:CONV_OUT], ACT.Copy, scale=weight).then_inc(first_tap, 1)

            def silu(i, w):
                act.wait_ge(conv_step, CONV_STEPS * (24 * a + i + 1))
                for c, (lo, hi) in enumerate(CHANNEL_SPANS):
                    pad = 2 * CONV_PAD * c // 2
                    dst = qkvz[:, bass.ds(i, 1), lo:hi].rearrange("p o c -> p (o c)")
                    ins = act.activation(dst, scratch[:, 2 + w % 2, lo + pad:hi + pad], ACT.Silu)
                ins.then_inc(conv_silu, 1)

            def body(b, first):
                for u in range(2):
                    unit = Unit(ph, u, 0 if first else b)
                    nxt = Unit(ph, u + 1, 0 if first else b)
                    for q in range(3):
                        w = 3 * u + q
                        i = w if first else 6 * b + w
                        round_part(nxt, q)
                        copy_padded(i, w, unit, q)
                        if not (first and w == 0):
                            silu(i - 1, w + 1)

            act.wait_ge(pad_zero, a + 1)
            body(0, True)
            with act.Fori(1, 4) as b:
                body(b, False)
            silu(23, 1)
            act.preload_act_table_set("natural_log_exp_and_others")
            for k in range(8, ph.units):
                unit = Unit(ph, k)
                nxt = Unit(ph, k + 1) if k + 1 < ph.units else None
                for q in range(3):
                    i = 3 * k + q
                    if nxt:
                        round_part(nxt, q)
                    if i >= 4 * HEADS:
                        continue
                    act.wait_ge(part_done[q], done(unit, q))
                    act.activation(qkvz[:, i], ps[PROJ_BANK[i % 3]][:, 0:T], ACT.Copy).then_inc(tile_used, 1)
                    for e in (2 * (i - 24), 2 * (i - 24) + 1):
                        act.wait_ge(ss_done, 16 * a + e + 1)
                        if e >= 2:
                            act.wait_ge(unit_ready, 16 * a + e - 1)
                        row = scratch[:, 2 + e % 2, 0:T]
                        steps.settle(act.activation(row, ps[e % 2][:, 0:T], ACT.Ln, bias=bias_eps[:, 0:1]))
                        act.activation(row, row, ACT.Exp, scale=-0.5).then_inc(r_ready, 1)
            def turned_values(heads):
                for h in heads:
                    act.wait_ge(tokT_done, 16 * a + h + 1)
                    act.activation(dn_v[:, :, h], ps[2 + h % 2][:, 0:T].rearrange("p (c e) -> p c e", c=NT), ACT.Copy).then_inc(tok_v, 1)

            turned_values(range(0, HEADS // 2))
            act.wait_ge(ab_in, a + 1)
            flat = lambda i: dn_small[:, i].rearrange("p c d h -> p (c d h)")
            steps.settle(act.activation(flat(SM_ABS), flat(SM_ABS), ACT.Exp, scale=-1.0))
            act.activation(flat(SM_B), flat(SM_B), ACT.Exp, scale=-1.0)
            act.activation(at_small[:, 0:16], rows[:, ROW_A_LOG + 16 * a:ROW_A_LOG + 16 * a + 16], ACT.Exp)
            act.activation(flat(SM_ABS), flat(SM_ABS), ACT.Ln, bias=ones[:, 0:1]).then_inc(ab_exp, 1)
            turned_values(range(HEADS // 2, HEADS))
            act.wait_ge(decay_in, a + 1)
            act.activation(flat(SM_EG), flat(SM_GC), ACT.Exp)
            act.activation(flat(SM_GLAST), flat(SM_TOTAL), ACT.Exp)
            act.activation(flat(SM_EKD), flat(SM_EKD), ACT.Exp).then_inc(decay_out, 1)

        def delta_net(layer):
            a = layer // 3

            def prepare(pair):
                for d in range(2):
                    e = work[d][W_Y][:]
                    act.wait_ge(pre_dve[d], N_PV * (6 * a + pair) + PV_MIN)
                    act.activation(e, e, ACT.Exp).then_inc(pre_act[d], 1)

            prepare(0)
            for pair in range(len(PAIRS)):
                g = 6 * a + pair
                for lev in range(LEVELS):
                    for d in range(2):
                        act.wait_ge(dn_mm[d], N_MM * g + mm_u(lev))
                        act.activation(work[d][W_U][:].rearrange("p h c -> p (h c)"), ps[4 * d + 2][:], ACT.Copy).then_inc(dn_act[d], 1)
                for d in range(2):
                    act.wait_ge(dn_mm[d], N_MM * g + MM_VN)
                    act.activation(work[d][W_VN][:].rearrange("p h c -> p (h c)"), ps[4 * d][:], ACT.Copy).then_inc(dn_act[d], 1)
                if pair + 1 < len(PAIRS):
                    prepare(pair + 1)
            act.activation(qkvz[:, 24:32].rearrange("p h t -> p (h t)"), qkvz[:, 24:32].rearrange("p h t -> p (h t)"),
                           ACT.Silu).then_inc(z_ready, 1)
            for d in range(2):
                act.wait_ge(dn_dve[d], N_DV * (6 * a + 6))
                act.wait_ge(dn_sum[d], (4 if d else 2) * (a + 1))

        def tail(layer, kind, out_ph):
            m = tail_index(layer)
            o = dn_o if kind == "a" else at_o
            for t in range(NT):
                act.activation(sq_tmp[:, t], o[:, t], ACT.Square).then_inc(osq_ready, 1)
            round_unit(Unit(out_ph, 0))
            for h in range(HEADS):
                row = scratch[:, h % 4, 0:T]
                if kind == "a":
                    act.wait_ge(on_ready, HEADS * layer + h + 1)
                else:
                    act.wait_ge(otr_ready, HEADS * m + h + 1)
                    if h >= 4:
                        act.wait_ge(oT_ready, oT_base(layer) + h - 3)
                    act.activation(row, ps[6 + h % 2][:, 0:T], ACT.Copy, scale=at_small[:, AT_NORM:AT_NORM + 1]).then_inc(on_ready, 1)
                    act.wait_ge(on_ready, HEADS * layer + h + 1)
                act.activation(xT_hi[:, h], row, ACT.Copy).then_inc(ohi_ready, 1)
                if h in (1, 5):
                    round_unit(Unit(out_ph, 1 + h // 5))
            nxt = following(Unit(out_ph, out_ph.units - 1))
            if nxt:
                round_unit(nxt)

        def attention(ph):
            act.wait_ge(lam_ready, 1)
            lam = at_small[:, AT_LAM:AT_LAM + 2]
            act.activation(lam, lam, ACT.Exp).then_inc(lam_exp, 1)
            dests = (at_q, at_k, at_v)
            for k in range(ph.units):
                unit = Unit(ph, k)
                for t in range(NT):
                    if k + 1 < ph.units:
                        round_part(Unit(ph, k + 1), t)
                    act.wait_ge(part_done[t], done(unit, t))
                    lo, end = 3 * P * k, 3 * P * (k + 1)
                    start = lo
                    while start < end:
                        stop = min(end, (start // D + 1) * D)
                        ins = act.activation(dests[start // D][:, t, start % D:start % D + stop - start],
                                             ps[PROJ_BANK[t]][:, start - lo:stop - lo], ACT.Copy)
                        start = stop
                    ins.then_inc(qkv_copied, 1)
            for h in range(HEADS):
                act.wait_ge(head_tr, 2 * h + 1)
                act.activation(qT[:, h], ps[h % 2][:, 0:T], ACT.Copy, scale=DH ** -0.5).then_inc(q_head, 1)
            items = NT * HEADS
            for i in range(items + 2):
                if i < items:
                    par, slot, keys = i % 2, i % PROBS, P if i % NT == 0 else T
                    act.wait_ge(max_done, i + 1)
                    if i >= PROBS:
                        act.wait_ge(pT_done, i - PROBS + 1)
                    for c in range(2):
                        m = at_small[:, AT_NEG_MAX + 2 * slot + c:AT_NEG_MAX + 2 * slot + c + 1]
                        total = at_small[:, AT_SUM + 2 * slot + c:AT_SUM + 2 * slot + c + 1]
                        ins = act.activation(prob[:, slot, c, 0:keys], ps[4 * par + c][:, 0:keys], ACT.Exp, bias=m, accum_out=total)
                    ins.then_inc(exp_done, 1)
                if i >= 2:
                    j = i - 2
                    par, keys = j % 2, P if j % NT == 0 else T
                    act.wait_ge(pT_done, j + 1)
                    if j >= 2:
                        act.wait_ge(ao_done, j - 1)
                    act.activation(probT[:, par, 0:keys], ps[4 * par + 2][:, 0:keys], ACT.Copy).then_inc(pT_copied, 1)
            act.wait_ge(ao_done, items)
            act.wait_ge(ao_copied, items)
            act.wait_ge(prob_done, items)
            act.wait_ge(cache_out, 32)

        def pooling(ph):
            round_unit(following(Unit(ph, 0)))
            layer = ph.index
            for k in range(KT):
                act.wait_ge(on_ready, KT * layer + k + 1)
                act.activation(xT_hi[:, k], scratch[:, k % 4, 0:T], ACT.Copy).then_inc(ohi_ready, 1)

        for r in range(NORMS):
            phs = by_stage[r]
            kind = phs[0].name[0]
            norm(r, to_pad=kind == "c")
            if kind == "f":
                ffn(phs[0])
            if kind == "a":
                proj_a(phs[0])
                delta_net(r // 3)
                tail(r // 3, "a", phs[1])
            if kind == "b":
                attention(phs[0])
                tail(r // 3, "b", phs[1])
            if kind == "c":
                pooling(phs[0])
        norm(NORMS)

    @block.vector
    def _(dve):
        steps = Steps(dve, dve_seq)

        def rest_part(unit, q):
            if q >= unit.parts:
                return
            w = unit.width(q)
            dve.wait_ge(hi_ready, unit.split_count(q))
            dve.tensor_tensor(split_lo[:, unit.slot, q, 0:w], raw[:, unit.slot, q, 0:w],
                              f32(split_hi[:, unit.slot, q, 0:w]), ALU.subtract).then_inc(lo_ready, 1)

        def rest_unit(unit):
            for q in range(3):
                rest_part(unit, q)

        def vectors(r):
            par, v0 = vec_of(r)
            dve.wait_ge(*mod_count("dve", mod_needed(r)))
            dve.wait_ge(*mod_count("act", mod_needed(r)))
            v = modv[:, par, v0:v0 + 3 * KT]
            b0 = COL_MOD_B + N_MOD * KT * (r // 3) + v0
            b = cols[:, b0:b0 + 3 * KT].rearrange("p (k o) -> p k o", o=1).to_broadcast([P, 3 * KT, 2])
            steps.settle(dve.tensor_tensor(v, v, b, ALU.add))

        def gates(r):
            if r:
                vectors(r)
            par, v0 = vec_of(r)
            gate = modv[:, par, v0 + 2 * KT:v0 + 3 * KT]
            if r % 3 != 1:
                steps.settle(dve.tensor_scalar(gate_col[:], gate, 0.5, None, ALU.mult))
            elif r == 7:
                cs = cols[:, COL_C_SCALE:COL_C_SCALE + KT].rearrange("p (k o) -> p k o", o=1).to_broadcast([P, KT, 2])
                steps.settle(dve.tensor_tensor(gate_col[:], gate, cs, ALU.mult))
            else:
                steps.settle(dve.tensor_copy(gate_col[:], gate))
            if r:
                dve.wait_ge(gate_mm, 4 * r)
            for c in range(2):
                i = ident[:].rearrange("p (o c) -> p o c", o=1).to_broadcast([P, KT, P])
                dve.tensor_tensor(diag[:, c], i, gate_col[:, :, c:c + 1].to_broadcast([P, KT, P]),
                                  ALU.mult).then_inc(diag_ready, 1)

        def scales(r):
            par, v0 = vec_of(r)
            steps.settle(dve.tensor_scalar(scale_col[:], modv[:, par, v0 + KT:v0 + 2 * KT], 1.0, None, ALU.add))
            g = cols[:, COL_NORM_G + KT * r:COL_NORM_G + KT * (r + 1)].rearrange("p (k o) -> p k o", o=1)
            dve.tensor_tensor(scale_col[:], scale_col[:], g.to_broadcast([P, KT, 2]), ALU.mult).then_inc(scale_ready, 1)

        def norm(r, to_pad=False):
            for t in range(NT):
                dve.wait_ge(rstd_ready, NT * r + t + 1)
                dve.tensor_scalar(xhat[:, t], x[:, t], rstd[:, t:t + 1], None, ALU.mult).then_inc(xhat_ready, 1)
            if r == 0:
                rest_part(Unit(phases[0], 0), 0)
                gates(0)
            if to_pad:
                return
            for k in range(KT):
                if r == 0 and k == KT // 2:
                    rest_part(Unit(phases[0], 0), 1)
                dve.wait_ge(xn_ready, xT_base(r) + k + 1)
                row = scratch[:, k % 4, 0:T]
                steps.settle(dve.tensor_copy(xT_hi[:, k], row))
                dve.tensor_tensor(xT_lo[:, k], row, f32(xT_hi[:, k]), ALU.subtract).then_inc(xT_ready, 1)
            if r == 0:
                rest_part(Unit(phases[0], 0), 2)

        def ffn(ph, r):
            f = ph.index
            s0 = FT * f

            def body(b, first, last):
                if last and r + 1 < NORMS:
                    gates(r + 1)
                for u in range(2):
                    k = u if first else ph.units - 2 + u if last else u
                    body_of = 0 if first or last else b
                    unit = Unit(ph, k, body_of)
                    nxt = following(unit) if (last and u == 1) else Unit(ph, k + 1, body_of)
                    j = unit.local
                    par = u % 2
                    if nxt:
                        rest_part(nxt, 0)
                        rest_part(nxt, 1)
                    dve.wait_ge(part_done[1], done(unit, 1))
                    dve.wait_ge(silu_done, s0 + j + 1)
                    dve.tensor_tensor(hidden[:, par], silu_g[:, par], ps[BANK_UP][:, 0:T], ALU.mult).then_inc(prod_done, 1)
                    dve.wait_ge(hid_hi_done, s0 + j + 1)
                    dve.tensor_tensor(hid_lo[:, par], hidden[:, par], f32(hid_hi[:, par]), ALU.subtract).then_inc(hid_done, 1)
                    if nxt:
                        rest_part(nxt, 2)
                    for step, m, slot, landed, layer in mod_steps(f, b, first, last):
                        if step == u:
                            mod_dve(dve, mod_raw[:, slot], mod_landed[slot], landed, m, layer, m - MOD_UNITS * layer)

            bodies(dve, FT // 2, body)

        def residual(r, last_unit):
            dve.wait_ge(gate_ready, 4 * r + 4)
            for i in range(2 * NT):
                t, half = divmod(i, 2)
                if half == 0 and t < NT - 1 and last_unit.phase.name != "c_in":
                    dve.wait_ge(sub_done, sub_base(r) + t + 1)
                elif half == 0:
                    for q in range(last_unit.parts):
                        dve.wait_ge(part_done[q], done(last_unit, q))
                span = slice(512 * half, 512 * half + 512)
                if i >= 3:
                    if (i - 3) % 2 == 0:
                        dve.wait_ge(res_pool, NT * r + (i - 3) // 2 + 1)
                    else:
                        dve.wait_ge(res_dve, NT * r + (i - 3) // 2 + 1)
                dve.tensor_tensor(res_tmp[:, i % 3], ps[i][:], gate_bc[:, min(t, 1), span], ALU.mult).then_inc(res_prod, 1)
                if half:
                    dve.wait_ge(res_prod, 6 * r + i + 1)
                    dve.tensor_tensor(x[:, t, span], x[:, t, span], res_tmp[:, i % 3], ALU.add).then_inc(res_dve, 1)

        def proj_a(ph):
            a = ph.index // 3

            def convolve(i, w):
                dve.wait_ge(first_tap, 24 * a + i + 1)
                for tap in range(1, CONV):
                    weight = cols[:, bass.ds(COL_CONV + 24 * CONV * a + CONV * i + tap, 1)]
                    for part, (lo, hi) in enumerate(CONV_PARTS):
                        src, dst = scratch[:, w % 2, lo + tap:hi + tap], scratch[:, 2 + w % 2, lo:hi]
                        if tap > 1:
                            dve.wait_ge(conv_step, CONV_STEPS * (24 * a + i) + len(CONV_PARTS) * (tap - 2) + part + 1)
                        dve.scalar_tensor_tensor(dst, src, weight, dst, ALU.mult, ALU.add).then_inc(conv_step, 1)

            def body(b, first):
                for u in range(2):
                    nxt = Unit(ph, u + 1, 0 if first else b)
                    for q in range(3):
                        w = 3 * u + q
                        rest_part(nxt, q)
                        convolve(w if first else 6 * b + w, w)

            body(0, True)
            with dve.Fori(1, 4) as b:
                body(b, False)

            def square(e):
                dve.wait_ge(conv_silu, 24 * a + (24 if e < 2 else e + 1))
                if e >= 2:
                    dve.wait_ge(ss_done, 16 * a + e - 1)
                dve.tensor_tensor(scratch[:, e % 2, 0:T], qkvz[:, e], qkvz[:, e], ALU.mult).then_inc(sq_ready, 1)

            def scale_unit(e):
                dve.wait_ge(r_ready, 16 * a + e + 1)
                row = scratch[:, 2 + e % 2, 0:T]
                if e < HEADS:
                    ins = dve.scalar_tensor_tensor(qkvz[:, e], qkvz[:, e], P ** -0.5, row, ALU.mult, ALU.mult)
                else:
                    ins = dve.tensor_tensor(qkvz[:, e], qkvz[:, e], row, ALU.mult)
                ins.then_inc(unit_ready, 1)

            square(0)
            square(1)
            for k in range(8, ph.units):
                nxt = Unit(ph, k + 1) if k + 1 < ph.units else None
                if nxt is None:
                    dve.wait_ge(part_done[2], done(Unit(ph, k), 2))
                    dve.tensor_copy(ab_rows[0:AB], ps[4][0:AB, 0:T]).then_inc(ab_rows_ready, 1)
                for q in range(3):
                    if nxt:
                        rest_part(nxt, q)
                    z = 3 * k + q - 24
                    if z < HEADS:
                        for e in (2 * z, 2 * z + 1):
                            scale_unit(e)
                            if e + 2 < 16:
                                square(e + 2)
            flat = lambda i: dn_small[:, i].rearrange("p c d h -> p (c d h)")
            by_c = lambda i: dn_small[:, i].rearrange("p c d h -> p c (d h)")
            dve.wait_ge(ab_turned, a + 1)
            ab = ps[4][:, 0:NT * AB].rearrange("p (c d s h) -> p c d s h", c=NT, d=2, s=2)
            for c in range(NT):
                dt = rows[:, ROW_DT + 16 * a:ROW_DT + 16 * a + 16].rearrange("p (d h) -> p d h", d=2)
                ins = dve.tensor_tensor(dn_small[:, SM_X, c], ab[:, c, :, 0], dt, ALU.add)
                steps.settle(dve.tensor_copy(dn_small[:, SM_B, c], ab[:, c, :, 1]))
            dve.scalar_tensor_tensor(flat(SM_ABS), flat(SM_X), -1.0, flat(SM_X), ALU.mult, ALU.max).then_inc(ab_in, 1)
            dve.wait_ge(ab_exp, a + 1)
            steps.settle(dve.scalar_tensor_tensor(flat(SM_X), flat(SM_X), 0.0, flat(SM_ABS), ALU.max, ALU.add))
            na = at_small[:, 0:16].rearrange("p (o c) -> p o c", o=1).to_broadcast([P, NT, 16])
            dve.scalar_tensor_tensor(by_c(SM_G), by_c(SM_X), -1.0, na, ALU.mult, ALU.mult).then_inc(g_ready, 1)
            steps.settle(dve.tensor_scalar(flat(SM_B), flat(SM_B), 1.0, None, ALU.add))
            steps.settle(dve.reciprocal(flat(SM_BETA), flat(SM_B)))
            dve.wait_ge(gc_done, a + 1)
            both = dn_small[:, SM_GC:SM_TOTAL + 1].rearrange("p i c d h -> p (i c d h)")
            steps.settle(dve.tensor_copy(both, ps[4][:, 0:4 * NT * HEADS]))
            dve.tensor_tensor(flat(SM_EKD), flat(SM_TOTAL), flat(SM_GC), ALU.subtract).then_inc(decay_in, 1)
            dve.wait_ge(decay_out, a + 1)
            dve.tensor_tensor(flat(SM_BEG), flat(SM_BETA), flat(SM_EG), ALU.mult).then_inc(small_ready, 1)
            dve.wait_ge(small_ready, a + 1)
            for h in range(HEADS):
                dve.wait_ge(tokT_done, 16 * a + HEADS + h + 1)
                dve.tensor_copy(dn_k[:, :, h], ps[2 + h % 2][:, 0:T].rearrange("p (c e) -> p c e", c=NT)).then_inc(tok_k, 1)

        def delta_net(layer):
            a = layer // 3

            def bank(d, i):
                return ps[4 * d + i][:].rearrange("p (h c) -> p h c", h=GROUP)

            def on(d, ins):
                ins.then_inc(dn_dve[d], 1)

            def steps_of_decay(pair):
                chunks, quad = PAIRS[pair]
                for d in range(2):
                    dve.tensor_tensor(work[d][W_Y][:], per_head(tri[:, d]), small(SM_G, chunks[d], d, quad),
                                      ALU.mult).then_inc(pre_dve[d], 1)

            def decay_exponents(pair):
                chunks, quad = PAIRS[pair]
                g = 6 * a + pair
                for d in range(2):
                    e = work[d][W_Y][:]
                    dve.wait_ge(pre_mm[d], N_PM * g + PM_D)
                    dve.tensor_tensor(e, bank(d, 2), small(SM_GC, chunks[d], d, quad), ALU.subtract).then_inc(pre_dve[d], 1)
                    dve.wait_ge(pre_dve[d], N_PV * g + PV_ARG)
                    dve.tensor_scalar(e, e, 0.0, None, ALU.min).then_inc(pre_dve[d], 1)

            def decayed_keys(pair):
                for d in range(2):
                    dve.wait_ge(pre_mm[d], N_PM * (6 * a + pair) + PM_KK)
                    dve.wait_ge(pre_pool[d], 6 * a + pair + 1)
                    dve.tensor_tensor(work[d][W_A][:], bank(d, 0), work[d][W_Y][:], ALU.mult).then_inc(pre_dve[d], 1)

            def decayed_queries(pair):
                for d in range(2):
                    dve.wait_ge(pre_mm[d], N_PM * (6 * a + pair) + PM_KQ)
                    dve.tensor_tensor(work[d][W_ATT][:], bank(d, 1), work[d][W_Y][:], ALU.mult).then_inc(pre_dve[d], 1)

            steps_of_decay(0)
            decay_exponents(0)
            decayed_keys(0)
            decayed_queries(0)
            for pair, (chunks, quad) in enumerate(PAIRS):
                g = 6 * a + pair
                hs = heads_of(quad)
                more = pair + 1 < len(PAIRS)
                mm = lambda d, n: dve.wait_ge(dn_mm[d], N_MM * g + n)
                own = lambda d, n: dve.wait_ge(dn_dve[d], N_DV * g + n)
                val = lambda which, d: small(which, chunks[d], d, quad)
                for lev in range(LEVELS):
                    for d in range(2):
                        mm(d, mm_y(lev))
                        if lev == 0:
                            dve.wait_ge(pre_dve[d], N_PV * g + PV_ATT)
                        on(d, dve.tensor_tensor(work[d][W_Y][:], bank(d, 0), val(SM_BETA, d), ALU.mult))
                    for d in range(2):
                        w = work[d]
                        if lev == 0:
                            own(d, dv_y(0))
                            on(d, dve.tensor_tensor(w[W_T][:], per_head(ident[:]), w[W_Y][:], ALU.subtract))
                        else:
                            mm(d, mm_z(lev))
                            steps_done = 4 if from_nothing(pair) and lev == LEVELS - 1 else 1
                            dve.tensor_tensor(w[W_T][:], w[W_T][:], bank(d, 1), ALU.subtract).then_inc(dn_dve[d], steps_done)
                if more:
                    steps_of_decay(pair + 1)
                for d in range(0 if from_nothing(pair) else 2):
                    w = work[d]
                    if pair and not writes_first(pair - 1, d):
                        dve.wait_ge(dn_sum[d], sum_count(a, pair - 1, d))
                    mm(d, MM_KS)
                    on(d, dve.tensor_tensor(w[W_E][:], bank(d, 3), val(SM_BEG, d), ALU.mult))
                    dve.wait_ge(dn_pool[d], N_PO * g + PO_VB)
                    own(d, DV_KS)
                    on(d, dve.tensor_tensor(w[W_VB][:], w[W_VB][:], w[W_E][:], ALU.subtract))
                for d in range(2):
                    w = work[d]
                    if not from_nothing(pair):
                        mm(d, MM_QS)
                        own(d, DV_R)
                        on(d, dve.tensor_tensor(w[W_E][:], bank(d, 2), val(SM_EG, d), ALU.mult))
                    mm(d, MM_VN)
                    dve.wait_ge(dn_act[d], N_AC * g + AC_VN)
                    on(d, dve.tensor_tensor(w[W_T][:], bank(d, 0), val(SM_EKD, d), ALU.mult))
                if more:
                    decay_exponents(pair + 1)
                for d in range(2):
                    w = work[d]
                    mm(d, MM_OI)
                    own(d, DV_VS)
                    dst = dn_o[:, chunks[d], hs] if writes_first(pair, d) else w[W_E][:]
                    if from_nothing(pair):
                        if pair and not writes_first(pair - 1, d):
                            dve.wait_ge(dn_sum[d], sum_count(a, pair - 1, d))
                        on(d, dve.tensor_copy(dst, bank(d, 1)))
                    else:
                        on(d, dve.tensor_tensor(dst, w[W_E][:], bank(d, 1), ALU.add))
                if more:
                    decayed_keys(pair + 1)
                for d in range(2):
                    mm(d, MM_DS)
                    dve.wait_ge(dn_pool[d], N_PO * g + PO_STATE)
                    if from_nothing(pair):
                        on(d, dve.tensor_copy(state[:, d, hs], bank(d, 3)))
                    else:
                        on(d, dve.tensor_tensor(state[:, d, hs], state[:, d, hs], bank(d, 3), ALU.add))
                if more:
                    decayed_queries(pair + 1)

        def sum_count(a, pair, d):
            per = [int(not writes_first(i, d)) for i in range(len(PAIRS))]
            return sum(per) * a + sum(per[:pair + 1])

        def tail(layer, kind, out_ph):
            m = tail_index(layer)
            o = dn_o if kind == "a" else at_o
            for t in range(NT):
                dve.wait_ge(osq_ready, NT * m + t + 1)
                dve.tensor_reduce(sumsq[:, HEADS * t:HEADS * t + HEADS], sq_tmp[:, t], AX.X, ALU.add).then_inc(oss_ready, 1)
            rest_part(Unit(out_ph, 0), 0)
            for t in range(NT):
                dve.wait_ge(orstd_ready, NT * m + t + 1)
                r = rstd[:, HEADS * t:HEADS * t + HEADS].rearrange("p (h o) -> p h o", o=1).to_broadcast([P, HEADS, P])
                dve.tensor_tensor(o[:, t], o[:, t], r, ALU.mult).then_inc(ohat_ready, 1)
            for h in range(HEADS):
                row = scratch[:, h % 4, 0:T]
                if kind == "a":
                    if h == 0:
                        dve.wait_ge(z_ready, layer // 3 + 1)
                    dve.wait_ge(otr_ready, HEADS * m + h + 1)
                    dve.scalar_tensor_tensor(row, ps[6 + h % 2][:, 0:T], cols[:, COL_A_NORM + layer // 3:COL_A_NORM + layer // 3 + 1],
                                             qkvz[:, 24 + h], ALU.mult, ALU.mult).then_inc(on_ready, 1)
                dve.wait_ge(ohi_ready, HEADS * layer + h + 1)
                dve.tensor_tensor(xT_lo[:, h], row, f32(xT_hi[:, h]), ALU.subtract).then_inc(oT_ready, 1)
                if h == 0:
                    rest_part(Unit(out_ph, 0), 1)
                    rest_part(Unit(out_ph, 0), 2)
                if h in (1, 5):
                    rest_unit(Unit(out_ph, 1 + h // 5))
                if h == 3 and kind == "a" and 3 * layer + 2 < NORMS:
                    gates(3 * layer + 2)
            nxt = following(Unit(out_ph, out_ph.units - 1))
            if nxt:
                rest_unit(nxt)

        def attention(ph):
            lam_rows = rows[:, ROW_LAM:ROW_LAM + 4 * DH].rearrange("p (a b c) -> p a b c", a=2, b=2)
            steps.settle(dve.tensor_tensor(lam_prod[:], lam_rows[:, :, 0], lam_rows[:, :, 1], ALU.mult))
            dve.tensor_reduce(at_small[:, AT_LAM:AT_LAM + 2], lam_prod[:], AX.X, ALU.add).then_inc(lam_ready, 1)
            dve.wait_ge(lam_exp, 1)
            neg_lam = at_small[:, AT_NEG_LAM:AT_NEG_LAM + 1]
            steps.settle(dve.tensor_tensor(neg_lam, at_small[:, AT_LAM + 1:AT_LAM + 2], at_small[:, AT_LAM:AT_LAM + 1], ALU.subtract))
            steps.settle(dve.tensor_scalar(neg_lam, neg_lam, -LAM_INIT, None, ALU.add))
            steps.settle(dve.tensor_scalar(at_small[:, AT_NORM:AT_NORM + 1], cols[:, COL_B_NORM:COL_B_NORM + 1],
                                           1.0 - LAM_INIT, None, ALU.mult))
            for k in range(ph.units):
                if k + 1 < ph.units:
                    rest_unit(Unit(ph, k + 1))
                if k == 5:
                    rotate()
            for h in range(HEADS):
                dve.wait_ge(head_tr, 2 * h + 2)
                dve.tensor_copy(kT[:, h], ps[2 + h % 2][:]).then_inc(k_head, 1)
            items = NT * HEADS
            for i in range(items + 3):
                if i < items:
                    par, slot, keys = i % 2, i % PROBS, P if i % NT == 0 else T
                    dve.wait_ge(score_done, i + 1)
                    for c in range(2):
                        m = at_small[:, AT_NEG_MAX + 2 * slot + c:AT_NEG_MAX + 2 * slot + c + 1]
                        ins = dve.tensor_reduce(m, ps[4 * par + c][:, 0:keys], AX.X, ALU.max, negate=True)
                    ins.then_inc(max_done, 1)
                if 1 <= i <= items:
                    j = i - 1
                    slot, keys = j % PROBS, P if j % NT == 0 else T
                    dve.wait_ge(exp_done, j + 1)
                    recip = at_small[:, AT_RECIP + 2 * slot:AT_RECIP + 2 * slot + 2]
                    second = at_small[:, AT_SCALED + slot:AT_SCALED + slot + 1]
                    steps.settle(dve.reciprocal(recip, at_small[:, AT_SUM + 2 * slot:AT_SUM + 2 * slot + 2]))
                    dve.tensor_scalar(second, recip[:, 1:2], neg_lam, None, ALU.mult)
                    p0, p1 = prob[:, slot, 0, 0:keys], prob[:, slot, 1, 0:keys]
                    steps.settle(dve.tensor_scalar(p0, p0, recip[:, 0:1], None, ALU.mult))
                    dve.scalar_tensor_tensor(p0, p1, second, p0, ALU.mult, ALU.add).then_inc(prob_done, 1)
                if i >= 3:
                    j = i - 3
                    dve.wait_ge(ao_done, j + 1)
                    dve.tensor_copy(at_o[:, j % NT, j // NT], ps[4 * (j % 2) + 3][:, 0:P]).then_inc(ao_copied, 1)

        def rotate():
            dve.wait_ge(qkv_copied, 6 * NT)
            groups = D // DH
            for t in range(1, NT):
                cos = rope_tab[:, t - 1, 0:1].to_broadcast([P, groups, DH])
                sin = rope_tab[:, t - 1, 1].rearrange("p (o b i f) -> p o b i f", o=1, b=2, i=2)
                for v in (at_q, at_k):
                    x3 = v[:, t].rearrange("p (g c) -> p g c", g=groups)
                    x4 = v[:, t].rearrange("p (g b i f) -> p g b i f", b=2, i=2, f=DH // 4)
                    r4 = rope_b[:].rearrange("p (g b i f) -> p g b i f", b=2, i=2, f=DH // 4)
                    dve.tensor_tensor(rope_a[:].rearrange("p (g c) -> p g c", g=groups), x3, cos, ALU.mult)
                    for i in range(2):
                        s4 = sin[:, :, :, i].to_broadcast([P, groups, 2, DH // 4])
                        ins = dve.tensor_tensor(r4[:, :, :, i], x4[:, :, :, 1 - i], s4, ALU.mult)
                    steps.settle(ins)
                    dve.tensor_tensor(v[:, t], rope_a[:], rope_b[:], ALU.add).then_inc(roped, 1)
                    dve.wait_ge(roped, 2 * (t - 1) + (1 if v is at_q else 2))

        def pooling(ph):
            layer = ph.index
            dve.wait_ge(count_in, 16)

            def rest(k):
                dve.wait_ge(ohi_ready, KT * layer + k + 1)
                dve.tensor_tensor(xT_lo[:, k], scratch[:, k % 4, 0:T], f32(xT_hi[:, k]), ALU.subtract).then_inc(oT_ready, 1)

            for k in range(KT):
                dve.wait_ge(hpad_ready, k + 1)
                a, b = pool_tmp[:, 0], pool_tmp[:, 1]
                steps.settle(dve.tensor_tensor(a[:, 1:POOL_W], hpad[:, k, 0:POOL_W - 1], hpad[:, k, 1:POOL_W], ALU.add))
                reach = 1
                for _ in range(k // 2):
                    lo, hi = 2 * reach, POOL_W - 2 * reach
                    steps.settle(dve.tensor_tensor(b[:, lo:hi], a[:, lo - reach:hi - reach], a[:, lo + reach:hi + reach], ALU.add))
                    a, b = b, a
                    reach *= 2
                mean = pool_tmp[:, 2, 0:POOL_OUT]
                steps.settle(dve.tensor_tensor(mean, a[:, POOL_PAD:POOL_PAD + POOL_OUT], inv_count[:, k // 2], ALU.mult))
                for c, (lo, hi) in enumerate(CHANNEL_SPANS):
                    gap = POOL_PAD * c
                    ins = dve.tensor_tensor(scratch[:, k % 4, lo:hi], mean[:, lo + gap:hi + gap],
                                            hpad[:, k, lo + gap + POOL_PAD:hi + gap + POOL_PAD], ALU.subtract)
                ins.then_inc(on_ready, 1)
                if k:
                    rest(k - 1)
                if k == KT // 2:
                    rest_unit(following(Unit(ph, 0)))
            rest(KT - 1)

        for m in range(MOD_PROLOGUE):
            if m == 0:
                dve.wait_ge(cond_ready, 1)
            mod_dve(dve, *mod_operand(m), m, 0, m)
        dve.wait_ge(consts_in, 16 * CONSTS)
        vectors(0)
        for r in range(NORMS):
            phs = by_stage[r]
            kind = phs[0].name[0]
            scales(r)
            norm(r, to_pad=kind == "c")
            if kind == "f":
                ffn(phs[0], r)
            if kind == "a":
                proj_a(phs[0])
                delta_net(r // 3)
                tail(r // 3, "a", phs[1])
            if kind == "b":
                attention(phs[0])
                tail(r // 3, "b", phs[1])
            if kind == "c":
                pooling(phs[0])
            if r + 1 < NORMS and kind in "bc":
                gates(r + 1)
            residual(r, Unit(phs[-1], phs[-1].units - 1))
        dve.wait_ge(rstd_ready, NT * NORMS + NT)
        dve.wait_ge(count_in, 16 * (stages > 7) + 16)
        for t in range(NT):
            steps.settle(dve.tensor_scalar(xhat[:, t], x[:, t], rstd[:, t:t + 1], None, ALU.mult))
            dve.tensor_tensor(xhat[:, t], xhat[:, t], final_row[:], ALU.mult).then_inc(y_ready, 1)

    @block.tensor
    def _(pe):
        def three(out, w_hi, w_lo, a_hi, a_lo, start, stop, weights_stationary=True):
            pairs = ((w_hi, a_hi), (w_hi, a_lo), (w_lo, a_hi))
            for i, (w, a) in enumerate(pairs if weights_stationary else ((w_hi, a_hi), (w_lo, a_hi), (w_hi, a_lo))):
                lhsT, rhs = (w, a) if weights_stationary else (a, w)
                ins = pe.matmul(out, lhsT, rhs, start=start and i == 0, stop=stop and i == 2)
            return ins

        def gate_rows(r):
            pe.wait_ge(diag_ready, 2 * r + 2)
            for i in range(4):
                if r:
                    pe.wait_ge(res_prod, 6 * (r - 1) + i + 1)
                d = diag[:, i // 2].rearrange("p k c -> p (k c)")
                pe.matmul(ps[i][:], ones[:], d[:, (i % 2) * 512:(i % 2) * 512 + 512], start=True, stop=True).then_inc(gate_mm, 1)

        def norm(r):
            if r:
                gate_rows(r)
            for first in (0, KT // 2):
                if first:
                    if r == 0:
                        gate_rows(0)
                    pe.wait_ge(gate_ready, 4 * r + 4)
                for t in range(NT):
                    if not first:
                        pe.wait_ge(xhat_ready, NT * r + t + 1)
                    for k in range(first, first + KT // 2):
                        ins = pe.transpose(ps[NORM_BANK[k]][:, t * P:(t + 1) * P], xhat[:, t, k * P:(k + 1) * P], ident[:])
                        if t == NT - 1:
                            ins.then_inc(tr_ready, 1)

        def ffn(ph):
            f = ph.index
            s0 = FT * f
            xb = xT_base(3 * (f // 2) + 2 * (f % 2))

            def down(unit, par, count, first, last):
                pe.wait_ge(hid_done, count)
                for t in range(NT):
                    for half in range(2):
                        c = slice(512 * half, 512 * half + 512)
                        tok = slice(t * P, (t + 1) * P)
                        ins = three(ps[2 * t + half][:], split_hi[:, unit.slot, 2, c], split_lo[:, unit.slot, 2, c],
                                    hid_hi[:, par, tok], hid_lo[:, par, tok], first, last, weights_stationary=False)
                    if last and t < NT - 1:
                        ins.then_inc(sub_done, 1)
                ins.then_inc(part_done[2], 1)

            def body(b, first, last):
                for u in range(2):
                    k = u if first else ph.units - 2 + u if last else u
                    body_of = 0 if first or last else b
                    unit = Unit(ph, k, body_of)
                    j = unit.local
                    if not (first and u == 0):
                        pe.wait_ge(silu_done, s0 + j)
                    for q, bank in ((0, BANK_GATE), (1, BANK_UP)):
                        pe.wait_ge(lo_ready, unit.split_count(q))
                        if q == 1 and not (first and u == 0 and f == 0):
                            pe.wait_ge(prod_done, s0 + j)
                        for kk in range(KT):
                            if first and u == 0 and q == 0:
                                pe.wait_ge(xT_ready, xb + kk + 1)
                            w = slice(kk * P, (kk + 1) * P)
                            ins = three(ps[bank][:, 0:T], split_hi[:, unit.slot, q, w], split_lo[:, unit.slot, q, w],
                                        xT_hi[:, kk], xT_lo[:, kk], kk == 0, kk == KT - 1)
                        ins.then_inc(part_done[q], 1)
                    if first and u == 0:
                        continue
                    before = Unit(ph, k - 1, body_of)
                    pe.wait_ge(lo_ready, before.split_count(2))
                    down(before, (u - 1) % 2, s0 + j, first and u == 1, False)
                    if last and u == 1:
                        down(unit, u, s0 + j + 1, False, True)

            bodies(pe, FT // 2, body)

        def proj_a(ph):
            a = ph.index // 3
            xb = xT_base(3 * ph.index + 1)

            def tile(i, w, unit, q):
                pe.wait_ge(lo_ready, unit.split_count(q))
                if not (isinstance(i, int) and i < 3):
                    pe.wait_ge(tile_used, 32 * a + i - 2)
                for k in range(KT):
                    if isinstance(i, int) and i == 0:
                        pe.wait_ge(xT_ready, xb + k + 1)
                    c = slice(k * P, (k + 1) * P)
                    ins = three(ps[PROJ_BANK[w % 3]][:, 0:T], split_hi[:, unit.slot, q, c], split_lo[:, unit.slot, q, c],
                                xT_hi[:, k], xT_lo[:, k], k == 0, k == KT - 1)
                ins.then_inc(part_done[q], 1)

            def body(b, first):
                for u in range(2):
                    unit = Unit(ph, u, 0 if first else b)
                    for q in range(3):
                        w = 3 * u + q
                        tile(w if first else 6 * b + w, w, unit, q)

            body(0, True)
            with pe.Fori(1, 4) as b:
                body(b, False)
            for k in range(8, ph.units):
                unit = Unit(ph, k)
                for q in (2, 0, 1) if k == ph.units - 1 else range(3):
                    i = 3 * k + q
                    if i < 4 * HEADS:
                        tile(i, i, unit, q)
                        for e in (2 * (i - 24), 2 * (i - 24) + 1):
                            pe.wait_ge(sq_ready, 16 * a + e + 1)
                            if e >= 2:
                                pe.wait_ge(r_ready, 16 * a + e - 1)
                            pe.matmul(ps[e % 2][:, 0:T], ones[:], scratch[:, e % 2, 0:T], start=True, stop=True).then_inc(ss_done, 1)
                        if k == ph.units - 1 and q == 0:
                            pe.wait_ge(ab_rows_ready, a + 1)
                            for t in range(NT):
                                ins = pe.transpose(ps[4][:, t * AB:(t + 1) * AB], ab_rows[0:AB, t * P:(t + 1) * P], ident[0:AB, 0:AB])
                            ins.then_inc(ab_turned, 1)
                        continue
                    pe.wait_ge(lo_ready, unit.split_count(q))
                    for kk in range(KT):
                        c = slice(kk * AB, (kk + 1) * AB)
                        ins = three(ps[4][0:AB, 0:T], split_hi[:, unit.slot, q, c], split_lo[:, unit.slot, q, c],
                                    xT_hi[:, kk], xT_lo[:, kk], kk == 0, kk == KT - 1)
                    ins.then_inc(part_done[2], 1)
            for h in range(2 * HEADS):
                tile_at = (16 + h) if h < HEADS else h
                if h == 0:
                    pe.wait_ge(conv_silu, 24 * a + 24)
                if h >= 2:
                    s, n = (tok_v, h - 1) if h - 2 < HEADS else (tok_k, h - 1 - HEADS)
                    pe.wait_ge(s, HEADS * a + n)
                if h == HEADS:
                    pe.wait_ge(unit_ready, 16 * a + 16)
                    pe.wait_ge(g_ready, a + 1)
                    for c in range(NT):
                        for d in range(2):
                            at = HEADS * (2 * c + d)
                            pe.matmul(ps[4][:, at:at + HEADS], tri[:, d], dn_small[:, SM_G, c, d], start=True, stop=True)
                    pe.matmul(ps[4][:, 48:96], ones[:], dn_small[:, SM_G].rearrange("p c d h -> p (c d h)"),
                              start=True, stop=True).then_inc(gc_done, 1)
                for c in range(NT):
                    ins = pe.transpose(ps[2 + h % 2][:, c * P:(c + 1) * P], qkvz[:, tile_at, c * P:(c + 1) * P], ident[:])
                ins.then_inc(tokT_done, 1)

        def delta_net(layer):
            a = layer // 3
            pe.wait_ge(tok_k, HEADS * a + HEADS)
            pe.wait_ge(tok_v, HEADS * a + HEADS)
            pe.wait_ge(tile_used, 32 * a + 32)
            pe.wait_ge(r_ready, 16 * a + 16)
            pe.wait_ge(state_set, a + 1)
            def four(d, b, lhsT, rhs, transpose=False, counts=dn_mm, steps_done=1):
                for h in range(GROUP):
                    dst = ps[4 * d + b][:, h * P:(h + 1) * P]
                    if transpose:
                        ins = pe.transpose(dst, lhsT(h), ident[:])
                    else:
                        ins = pe.matmul(dst, lhsT(h), rhs(h), start=True, stop=True)
                ins.then_inc(counts[d], steps_done)

            def q_of(pair, d, h):
                chunks, quad = PAIRS[pair]
                return qkvz[:, GROUP * quad + h, chunks[d] * P:(chunks[d] + 1) * P]

            def k_of(pair, d, h):
                chunks, quad = PAIRS[pair]
                return qkvz[:, HEADS + GROUP * quad + h, chunks[d] * P:(chunks[d] + 1) * P]

            def decay_sums(pair):
                g = 6 * a + pair
                for d in range(2):
                    pe.wait_ge(pre_dve[d], N_PV * g + PV_G4)
                    if pair:
                        pe.wait_ge(dn_dve[d], N_DV * (g - 1) + DV_QS)
                    pe.matmul(ps[4 * d + 2][:], ones[:], work[d][W_Y][:].rearrange("p h c -> p (h c)"),
                              start=True, stop=True).then_inc(pre_mm[d], 1)

            def key_maps(pair):
                for d in range(2):
                    if pair:
                        pe.wait_ge(dn_dve[d], N_DV * (6 * a + pair - 1) + DV_VS)
                    four(d, 0, lambda h: k_of(pair, d, h), lambda h: k_of(pair, d, h), counts=pre_mm)

            def query_maps(pair):
                for d in range(2):
                    if pair:
                        pe.wait_ge(dn_dve[d], N_DV * (6 * a + pair - 1) + DV_O)
                    four(d, 1, lambda h: k_of(pair, d, h), lambda h: q_of(pair, d, h), counts=pre_mm)

            decay_sums(0)
            key_maps(0)
            query_maps(0)
            for pair, (chunks, quad) in enumerate(PAIRS):
                g = 6 * a + pair
                dv = lambda d, n: pe.wait_ge(dn_dve[d], N_DV * g + n)
                po = lambda d, n: pe.wait_ge(dn_pool[d], N_PO * g + n)
                ac = lambda d, n: pe.wait_ge(dn_act[d], N_AC * g + n)

                def y_product(d, lev):
                    w = work[d]
                    po(d, po_m(lev))
                    if lev:
                        dv(d, dv_t(lev - 1))
                    if lev:
                        four(d, 0, lambda h: w[W_MASK + lev % 2][:, h], lambda h: w[W_T][:, h])
                    else:
                        four(d, 0, lambda h: w[W_MASK][:, h], None, transpose=True)

                def u_transpose(d, lev):
                    dv(d, dv_t(lev))
                    if lev:
                        ac(d, ac_u(lev - 1))
                    four(d, 2, lambda h: work[d][W_T][:, h], None, transpose=True,
                         steps_done=3 if from_nothing(pair) and lev == LEVELS - 1 else 1)

                pre = lambda d, n: pe.wait_ge(pre_dve[d], N_PV * g + n)
                for d in range(2):
                    pre(d, PV_A)
                    y_product(d, 0)
                for lev in range(1, LEVELS):
                    for d in range(2):
                        y_product(d, lev)
                        u_transpose(d, lev - 1)
                    for d in range(2):
                        dv(d, dv_y(lev))
                        ac(d, ac_u(lev - 1))
                        pre(d, PV_ATT)
                        four(d, 1, lambda h: work[d][W_U][:, h], lambda h: work[d][W_Y][:, h])
                for d in range(2):
                    u_transpose(d, LEVELS - 1)
                    if from_nothing(pair):
                        continue
                    if pair in (2, 3):
                        pe.wait_ge(state_in, 16 * (4 * a + 2 * quad + 2))
                    four(d, 3, lambda h: k_of(pair, d, h), lambda h: state[:, d, GROUP * quad + h])
                for d in range(2):
                    ac(d, ac_u(LEVELS - 1))
                    if from_nothing(pair):
                        po(d, PO_VB)
                        continue
                    four(d, 2, lambda h: q_of(pair, d, h), lambda h: state[:, d, GROUP * quad + h])
                for d in range(2):
                    dv(d, DV_R)
                    four(d, 0, lambda h: work[d][W_U][:, h], lambda h: work[d][W_VB][:, h])
                if pair + 1 < len(PAIRS):
                    decay_sums(pair + 1)
                for d in range(2):
                    ac(d, AC_VN)
                if pair + 1 < len(PAIRS):
                    key_maps(pair + 1)
                for d in range(2):
                    four(d, 1, lambda h: work[d][W_ATT][:, h], lambda h: work[d][W_VN][:, h])
                for d in range(2):
                    dv(d, DV_VS)
                    four(d, 3, lambda h: dn_k[:, chunks[d], GROUP * quad + h], lambda h: work[d][W_T][:, h])
                if pair + 1 < len(PAIRS):
                    query_maps(pair + 1)

        def tail(layer, out_ph, o):
            m = tail_index(layer)
            pe.wait_ge(ohat_ready, NT * m + NT)

            def turn(h):
                if h >= 2:
                    pe.wait_ge(on_ready, HEADS * layer + h - 1)
                for t in range(NT):
                    ins = pe.transpose(ps[6 + h % 2][:, t * P:(t + 1) * P], o[:, t, h], ident[:])
                ins.then_inc(otr_ready, 1)

            turn(0)
            turn(1)
            for k in range(HEADS):
                unit, q = Unit(out_ph, k // 3), k % 3
                pe.wait_ge(oT_ready, oT_base(layer) + k + 1)
                pe.wait_ge(lo_ready, unit.split_count(q))
                for t in range(NT):
                    tok = slice(t * P, (t + 1) * P)
                    for half in range(2):
                        c = slice(512 * half, 512 * half + 512)
                        ins = three(ps[2 * t + half][:], split_hi[:, unit.slot, q, c], split_lo[:, unit.slot, q, c],
                                    xT_hi[:, k, tok], xT_lo[:, k, tok], k == 0, k == HEADS - 1, weights_stationary=False)
                    if k == HEADS - 1 and t < NT - 1:
                        ins.then_inc(sub_done, 1)
                ins.then_inc(part_done[q], 1)
                if k + 2 < HEADS:
                    turn(k + 2)

        def attention(ph):
            xb = xT_base(3 * ph.index + 1)
            for k in range(ph.units):
                unit = Unit(ph, k)
                pe.wait_ge(lo_ready, unit.split_count(2))
                for t in range(NT):
                    if NT * k + t >= 3:
                        pe.wait_ge(qkv_copied, NT * k + t - 2)
                    tok = slice(t * P, (t + 1) * P)
                    for kk in range(KT):
                        if k == 0 and t == 0:
                            pe.wait_ge(xT_ready, xb + kk + 1)
                        c = slice(kk * P, (kk + 1) * P)
                        ins = three(ps[PROJ_BANK[t]][:, 0:T].rearrange("p (q c) -> p q c", q=3), split_hi[:, unit.slot, :, c],
                                    split_lo[:, unit.slot, :, c], xT_hi[:, kk, tok], xT_lo[:, kk, tok],
                                    kk == 0, kk == KT - 1, weights_stationary=False)
                    ins.then_inc(part_done[t], 1)
            pe.wait_ge(roped, 4)
            pe.wait_ge(past_in, 32)
            for h in range(HEADS):
                c = slice(h * P, (h + 1) * P)
                if h >= 2:
                    pe.wait_ge(q_head, h - 1)
                    pe.wait_ge(k_head, h - 1)
                for t in range(NT):
                    ins = pe.transpose(ps[h % 2][:, t * P:(t + 1) * P], at_q[:, t, c], ident[:])
                ins.then_inc(head_tr, 1)
                for t in range(NT + 1):
                    src = at_k[:, t, c] if t < NT else past_k[:, c]
                    ins = pe.transpose(ps[2 + h % 2][:, t * P:(t + 1) * P], src, ident[:])
                ins.then_inc(head_tr, 1)
            pe.wait_ge(q_head, HEADS)
            pe.wait_ge(k_head, HEADS)
            items = NT * HEADS
            for i in range(items + 3):
                if i < items:
                    h, t, par = i // NT, i % NT, i % 2
                    if i >= 2:
                        pe.wait_ge(exp_done, i - 1)
                    keys = slice(0, P) if t == 0 else slice(P, T + PAST)
                    n = keys.stop - keys.start
                    for c in range(2):
                        half = slice(DH * c, DH * c + DH)
                        ins = pe.matmul(ps[4 * par + c][:, 0:n], qT[half, h, t * P:(t + 1) * P], kT[half, h, keys], start=True, stop=True)
                    ins.then_inc(score_done, 1)
                if 2 <= i < items + 2:
                    j = i - 2
                    par, tiles = j % 2, 1 if j % NT == 0 else NT
                    pe.wait_ge(prob_done, j + 1)
                    if j >= 2:
                        pe.wait_ge(pT_copied, j - 1)
                    for b in range(tiles):
                        ins = pe.transpose(ps[4 * par + 2][:, b * P:(b + 1) * P], prob[:, j % PROBS, 0, b * P:(b + 1) * P], ident[:])
                    ins.then_inc(pT_done, 1)
                if i >= 3:
                    j = i - 3
                    h, t, par = j // NT, j % NT, j % 2
                    pe.wait_ge(pT_copied, j + 1)
                    if j >= 2:
                        pe.wait_ge(ao_copied, j - 1)
                    c = slice(h * P, (h + 1) * P)
                    values = [at_v[:, 0, c]] if t == 0 else [at_v[:, 1, c], at_v[:, 2, c], past_v[:, c]]
                    for b, v in enumerate(values):
                        ins = pe.matmul(ps[4 * par + 3][:, 0:P], probT[:, par, b * P:(b + 1) * P], v, start=b == 0, stop=b == len(values) - 1)
                    ins.then_inc(ao_done, 1)

        def pooling(ph):
            pe.wait_ge(hpad_ready, KT)
            unit = Unit(ph, 0)
            for g in range(4):
                q, side = g // 2, g % 2
                pe.wait_ge(lo_ready, unit.split_count(q))
                pe.wait_ge(oT_ready, oT_base(ph.index) + 2 * g + 2)
                for t in range(NT):
                    tok = slice(t * P, (t + 1) * P)
                    for kk in range(2):
                        c = slice(512 * side + 256 * kk, 512 * side + 256 * kk + 256)
                        ins = three(ps[2 * t + q][:, 256 * side:256 * side + 256], split_hi[:, unit.slot, q, c],
                                    split_lo[:, unit.slot, q, c], xT_hi[:, 2 * g + kk, tok], xT_lo[:, 2 * g + kk, tok],
                                    kk == 0, kk == 1, weights_stationary=False)
                if side:
                    ins.then_inc(part_done[q], 1)


        pe.wait_ge(consts_in, 16 * CONSTS)
        pe.wait_ge(pool_init, 1)
        for r in range(NORMS):
            phs = by_stage[r]
            kind = phs[0].name[0]
            norm(r)
            if kind == "f":
                ffn(phs[0])
            if kind == "a":
                proj_a(phs[0])
                delta_net(r // 3)
                tail(r // 3, phs[1], dn_o)
            if kind == "b":
                attention(phs[0])
                tail(r // 3, phs[1], at_o)
            if kind == "c":
                pooling(phs[0])

    block.__exit__(None, None, None)


def shape_constants():
    i, j = np.meshgrid(np.arange(P), np.arange(P), indexing="ij")
    forward = (i <= j).astype(np.float32)
    tri = np.stack([forward, forward.T], axis=1)
    levels = []
    for lev in range(LEVELS):
        s = 1 << lev
        levels.append((((j // s) % 2 == 1) & (i // s == j // s - 1)).astype(np.float32))
    levels = np.stack(levels, axis=1)
    level_mask = np.stack([levels, levels.transpose(2, 1, 0)], axis=1)
    nf = DH // 4
    inv = (np.float32(10000.0) ** (-np.arange(nf, dtype=np.float32) / np.float32(nf))).astype(np.float32)
    tok = np.arange(TS)
    row = (tok // 64).astype(np.float32)[:, None] * inv
    col = (tok % 64).astype(np.float32)[:, None] * inv
    c = np.concatenate([np.cos(row), np.cos(row), np.cos(col), np.cos(col)], axis=1)
    s = np.concatenate([-np.sin(row), np.sin(row), -np.sin(col), np.sin(col)], axis=1)
    rope = np.stack([c, s], axis=1).astype(np.float32).reshape(2, P, 2, DH).transpose(1, 0, 2, 3)
    counts = np.zeros((4, POOL_OUT), np.float32)
    for g, w in enumerate(POOL_WINDOWS):
        for lo, n in ((0, TP), (TP + POOL_PAD, TS)):
            t = np.arange(n)
            counts[g, lo:lo + n] = 1.0 / (np.clip(t + w // 2, 0, n) - np.clip(t - w // 2, 0, n))
    f = np.ascontiguousarray
    return {"ident": np.eye(P, dtype=np.float32), "tri": f(tri), "level_mask": f(level_mask), "rope_tab": f(rope),
            "inv_count": f(counts.reshape(1, 4 * POOL_OUT))}


def lay_out(a):
    f = np.ascontiguousarray
    a = {k: np.asarray(v) for k, v in a.items()}
    z = shape_constants()
    by_tile = lambda w, n: w.reshape(KT, P, n, P).transpose(2, 1, 0, 3).reshape(n, P, PART)
    ffn = []
    for i in range(DEPTH):
        for h in range(2):
            parts = [by_tile(a["ffn_wg"][i, h], FT), by_tile(a["ffn_wu"][i, h], FT), a["ffn_wd"][i, h].reshape(FT, P, D)]
            ffn.append(np.concatenate(parts, axis=2))
    z["ffn_w"] = np.stack(ffn)
    z["mod_w"] = np.stack([w.T.reshape(MOD_UNITS, MOD_TILES, P, D).transpose(0, 2, 1, 3)
                           .reshape(MOD_UNITS, P, MOD_TILES * D) for w in a["w_mod"]])
    a_in = np.zeros((2, 11, P, 3 * PART), np.float32)
    for s in range(2):
        tiles = by_tile(a["a_w_in"][s][:, :4 * D], 4 * KT)
        a_in[s].reshape(11, P, 3, PART)[:10] = tiles[:30].reshape(10, 3, P, PART).transpose(0, 2, 1, 3)
        a_in[s, 10].reshape(P, 3, PART)[:, :2] = tiles[30:].transpose(1, 0, 2)
        a_in[s, 10, :, 2 * PART:2 * PART + KT * AB] = a["a_w_in"][s][:, 4 * D:].reshape(KT, P, AB).transpose(1, 0, 2).reshape(P, KT * AB)
    z["a_in_w"] = a_in
    rows_of = lambda w: f(w.reshape(KT, P, D).transpose(1, 0, 2).reshape(P, KT * D))
    z["a_out_w"] = np.stack([rows_of(w) for w in a["a_w_out"]])
    z["b_out_w"] = rows_of(a["b_w_out"][0])
    z["b_in_w"] = f(by_tile(a["b_w_qkv"][0], 24).reshape(8, 3, P, PART).transpose(0, 2, 1, 3).reshape(8, P, 3 * PART))
    z["c_w"] = f(a["c_w_pool"][0].reshape(4, 2, P, 256).transpose(2, 0, 1, 3).reshape(P, 2 * PART))
    chan = lambda v: v.reshape(-1, P).T
    z["cond"] = f(np.concatenate([a["c_ctx"], a["c"][0]])[None])
    conv = np.concatenate([a["a_conv"][s].reshape(CONV, 24, P).transpose(2, 1, 0).reshape(P, 24 * CONV) for s in range(2)], axis=1)
    z["cols"] = f(np.concatenate([chan(a["norm_g"]), chan(a["b_mod"]), conv, a["a_norm_g"].T, a["b_norm_g"].T,
                                  chan(a["c_scale"])], axis=1))
    z["rows"] = f(np.concatenate([a["a_A_log"].reshape(-1), a["a_dt_bias"].reshape(-1), a["b_lam"].reshape(-1)])[None])
    z["final_g"] = f(a["final_g"][None])
    z["x_prompt"], z["x_sample"] = f(a["x_prompt"][0]), f(a["x_sample"][0])
    z["state_a"] = f(a["state_a"][0])
    z["past_k"], z["past_v"] = f(a["cache_k"][0, 0].reshape(PAST, D)), f(a["cache_v"][0, 0].reshape(PAST, D))
    return z


OUTS = (("y_prompt", (TP, D)), ("y_sample", (TS, D)), ("state", (2, 2, HEADS, P, P)), ("cache_k", (TP, D)), ("cache_v", (TP, D)))


def program(nc, arrays, stages=3 * DEPTH):
    inp = {n: nc.dram_tensor(n, list(v.shape), F32, kind="ExternalInput").ap() for n, v in arrays.items()}
    out = {n: nc.dram_tensor("out_" + n, list(s), F32, kind="ExternalOutput").ap() for n, s in OUTS}
    build(nc, inp, out, stages)


def kernel(**inputs):
    import concourse.bacc as bacc
    from concourse.bass_utils import run_bass_kernel_spmd

    arrays = lay_out(inputs)
    nc = bacc.Bacc("TRN2", target_bir_lowering=False, num_devices=1)
    program(nc, arrays)
    r = run_bass_kernel_spmd(nc, [arrays], core_ids=[0]).results[0]
    return (r["out_y_prompt"].reshape(1, TP, D), r["out_y_sample"].reshape(1, TS, D),
            r["out_state"].reshape(1, 2, 2, HEADS, P, P), r["out_cache_k"].reshape(1, 1, TP, HEADS, P),
            r["out_cache_v"].reshape(1, 1, TP, HEADS, P))
```
